# Optimizing a Trainium2 kernel written in Bass

```python
import math
import jax, jax.numpy as jnp
from jax import lax
import numpy as np

D_MODEL = 1024
BATCH = 1
SEQ = 1024
DEPTH = 2

N_MIXERS = 4
HEAD_DIM = 64
N_HEADS = D_MODEL // HEAD_DIM
D_FF = 4 * D_MODEL
Q_BLOCK = 128
ROPE_THETA = 500000.0
ROT_DIM = HEAD_DIM // 4
RMS_EPS = 1e-6
NEG_INF = -1e30
FORCE_SCORE = 1e9
POOL_WINDOWS = (2, 4, 8, 16)
POOL_GROUP = D_MODEL // len(POOL_WINDOWS)
CONV_WIDTH = 3
NSA_KV_HEADS = 4
NSA_GROUP = N_HEADS // NSA_KV_HEADS
CMP_BLOCK = 32
CMP_STRIDE = 16
SLC_BLOCK = 64
SLC_TOPK = 16
WIN = 512
CMP_HIDDEN = 256

kernel_name = "hybrid_fox_pool_conv_nsa_trunk"

def rmsnorm(x, g):
    xf = x.astype(jnp.float32)
    y = xf * lax.rsqrt(jnp.mean(xf * xf, axis=-1, keepdims=True) + RMS_EPS)
    return (y * g.astype(jnp.float32)).astype(x.dtype)

def rope_tables(positions):
    inv = ROPE_THETA ** (-jnp.arange(0, ROT_DIM, 2, dtype=jnp.float32) / ROT_DIM)
    ang = positions.astype(jnp.float32)[:, None] * inv[None, :]
    return jnp.cos(ang), jnp.sin(ang)

def apply_partial_rope(x, cos, sin):
    half = ROT_DIM // 2
    x1, x2, xp = x[..., :half], x[..., half:ROT_DIM], x[..., ROT_DIM:]
    c = cos[None, :, None, :].astype(x.dtype)
    s = sin[None, :, None, :].astype(x.dtype)
    return jnp.concatenate([x1 * c - x2 * s, x2 * c + x1 * s, xp], axis=-1)

def sq_relu_mlp(h, w1, w2):
    return jnp.square(jax.nn.relu(h @ w1)) @ w2

def fox_attention(h, w_qkv, w_f, b_f, w_o):
    B, S, D = h.shape
    q, k, v = jnp.split(h @ w_qkv, 3, axis=-1)
    q = q.reshape(B, S, N_HEADS, HEAD_DIM)
    k = k.reshape(B, S, N_HEADS, HEAD_DIM)
    v = v.reshape(B, S, N_HEADS, HEAD_DIM)
    log_f = jax.nn.log_sigmoid((h @ w_f + b_f).astype(jnp.float32))
    cum = jnp.cumsum(log_f, axis=1)
    cum_t = cum.transpose(0, 2, 1)
    nblk = S // Q_BLOCK
    scale = HEAD_DIM ** -0.5
    key_pos = jnp.arange(S, dtype=jnp.int32)
    q_blocks = q.reshape(B, nblk, Q_BLOCK, N_HEADS, HEAD_DIM).swapaxes(0, 1)
    c_blocks = cum.reshape(B, nblk, Q_BLOCK, N_HEADS).swapaxes(0, 1)
    starts = jnp.arange(nblk, dtype=jnp.int32) * Q_BLOCK

    def block(args):
        q_i, c_i, s0 = args
        logits = jnp.einsum('bqhd,bkhd->bhqk', q_i, k, preferred_element_type=jnp.float32) * scale
        logits = logits + (c_i.transpose(0, 2, 1)[..., :, None] - cum_t[..., None, :])
        qpos = s0 + jnp.arange(Q_BLOCK, dtype=jnp.int32)
        mask = key_pos[None, :] <= qpos[:, None]
        p = jax.nn.softmax(jnp.where(mask, logits, NEG_INF), axis=-1)
        return jnp.einsum('bhqk,bkhd->bqhd', p.astype(v.dtype), v)

    o = lax.map(block, (q_blocks, c_blocks, starts))
    return o.swapaxes(0, 1).reshape(B, S, D) @ w_o

def pool_mixer(h, w_pool, pool_scale):
    B, S, D = h.shape
    hf = h.astype(jnp.float32)
    cs = jnp.concatenate([jnp.zeros((B, 1, D), jnp.float32), jnp.cumsum(hf, axis=1)], axis=1)
    t = jnp.arange(S, dtype=jnp.int32)
    diffs = []
    for g, w in enumerate(POOL_WINDOWS):
        sl = slice(g * POOL_GROUP, (g + 1) * POOL_GROUP)
        lo = jnp.maximum(t + 1 - w, 0)
        cnt = (t + 1 - lo).astype(jnp.float32)
        mean = (cs[:, 1:, sl] - cs[:, lo, sl]) / cnt[None, :, None]
        diffs.append(mean - hf[..., sl])
    d = jnp.stack(diffs, axis=2).astype(h.dtype)
    y = jnp.einsum('bsgi,gio->bsgo', d, w_pool).reshape(B, S, D)
    return y * pool_scale

def short_conv_mixer(h, w_in, conv_w, w_out):
    B, S, D = h.shape
    b_gate, c_gate, u = jnp.split(h @ w_in, 3, axis=-1)
    z = c_gate * u
    zp = jnp.pad(z, ((0, 0), (CONV_WIDTH - 1, 0), (0, 0)))
    conv = conv_w[0] * zp[:, 0:S]
    for j in range(1, CONV_WIDTH):
        conv = conv + conv_w[j] * zp[:, j:j + S]
    return (b_gate * conv) @ w_out

def nsa_attention(h, cos, sin, w_in, pe_k, w1_k, w2_k, pe_v, w1_v, w2_v, w_o):
    B, S, D = h.shape
    qd = N_HEADS * HEAD_DIM
    kvd = NSA_KV_HEADS * HEAD_DIM
    proj = h @ w_in
    q = proj[..., :qd].reshape(B, S, N_HEADS, HEAD_DIM)
    kv = proj[..., qd:qd + 6 * kvd].reshape(B, S, 6, NSA_KV_HEADS, HEAD_DIM)
    gates = jax.nn.sigmoid(proj[..., qd + 6 * kvd:].astype(jnp.float32)).reshape(B, S, 3, NSA_KV_HEADS, NSA_GROUP)
    k_cmp_raw, v_cmp_raw = kv[:, :, 0], kv[:, :, 1]
    k_slc, v_slc = apply_partial_rope(kv[:, :, 2], cos, sin), kv[:, :, 3]
    k_win, v_win = apply_partial_rope(kv[:, :, 4], cos, sin), kv[:, :, 5]
    q = apply_partial_rope(q, cos, sin).reshape(B, S, NSA_KV_HEADS, NSA_GROUP, HEAD_DIM)

    n_cmp = (S - CMP_BLOCK) // CMP_STRIDE + 1
    cmp_idx = np.arange(n_cmp)[:, None] * CMP_STRIDE + np.arange(CMP_BLOCK)[None, :]
    cmp_end = cmp_idx[:, -1]

    def compress(raw, pe, w1, w2):
        blocks = raw[:, cmp_idx] + pe[None, None, :, None, :]
        flat = blocks.transpose(0, 1, 3, 2, 4).reshape(B, n_cmp, NSA_KV_HEADS, CMP_BLOCK * HEAD_DIM)
        return jax.nn.gelu(flat @ w1) @ w2

    k_c = apply_partial_rope(compress(k_cmp_raw, pe_k, w1_k, w2_k), cos[cmp_end], sin[cmp_end])
    v_c = compress(v_cmp_raw, pe_v, w1_v, w2_v)
    cmp_end_j = jnp.asarray(cmp_end, dtype=jnp.int32)

    n_slc = S // SLC_BLOCK
    n_sel = min(SLC_TOPK, n_slc)
    slc_start = np.arange(n_slc) * SLC_BLOCK
    ci = np.arange(n_cmp)[:, None] * CMP_STRIDE
    overlap = jnp.asarray(((ci < slc_start[None, :] + SLC_BLOCK) & (ci + CMP_BLOCK > slc_start[None, :])).astype(np.float32))
    ks_blk = k_slc.reshape(B, n_slc, SLC_BLOCK, NSA_KV_HEADS, HEAD_DIM).transpose(0, 3, 1, 2, 4)
    vs_blk = v_slc.reshape(B, n_slc, SLC_BLOCK, NSA_KV_HEADS, HEAD_DIM).transpose(0, 3, 1, 2, 4)
    b_ix = jnp.arange(B)[:, None, None, None]
    h_ix = jnp.arange(NSA_KV_HEADS)[None, None, :, None]
    blk_ids = jnp.arange(n_slc, dtype=jnp.int32)[None, :]

    pad = jnp.zeros((B, WIN, NSA_KV_HEADS, HEAD_DIM), k_win.dtype)
    k_win_p = jnp.concatenate([pad, k_win], axis=1)
    v_win_p = jnp.concatenate([pad, v_win], axis=1)

    nblk = S // Q_BLOCK
    scale = HEAD_DIM ** -0.5
    q_blocks = q.reshape(B, nblk, Q_BLOCK, NSA_KV_HEADS, NSA_GROUP, HEAD_DIM).swapaxes(0, 1)
    g_blocks = gates.reshape(B, nblk, Q_BLOCK, 3, NSA_KV_HEADS, NSA_GROUP).swapaxes(0, 1)
    starts = jnp.arange(nblk, dtype=jnp.int32) * Q_BLOCK

    def block(args):
        q_i, g_i, s0 = args
        qpos = s0 + jnp.arange(Q_BLOCK, dtype=jnp.int32)
        sc = jnp.einsum('bqkgd,bnkd->bqkgn', q_i, k_c, preferred_element_type=jnp.float32) * scale
        cmask = cmp_end_j[None, :] <= qpos[:, None]
        sc = jnp.where(cmask[None, :, None, None, :], sc, NEG_INF)
        p_c = jnp.where(cmask.any(-1)[None, :, None, None, None], jax.nn.softmax(sc, axis=-1), 0.0)
        o_c = jnp.einsum('bqkgn,bnkd->bqkgd', p_c.astype(v_c.dtype), v_c)
        imp = jnp.einsum('bqkgn,nj->bqkj', p_c, overlap)
        cur = (qpos // SLC_BLOCK)[:, None]
        forced = (blk_ids == 0) | (blk_ids == cur) | (blk_ids == cur - 1)
        valid = blk_ids * SLC_BLOCK <= qpos[:, None]
        imp = jnp.where(forced[None, :, None, :], FORCE_SCORE, imp)
        imp = jnp.where(valid[None, :, None, :], imp, NEG_INF)
        top_val, top_idx = lax.top_k(imp, n_sel)
        ks = ks_blk[b_ix, h_ix, top_idx]
        vs = vs_blk[b_ix, h_ix, top_idx]
        ss = jnp.einsum('bqkgd,bqknld->bqkgnl', q_i, ks, preferred_element_type=jnp.float32) * scale
        tok = top_idx[..., None] * SLC_BLOCK + jnp.arange(SLC_BLOCK, dtype=jnp.int32)
        smask = (top_val > 0.5 * NEG_INF)[..., None] & (tok <= qpos[None, :, None, None, None])
        ss = jnp.where(smask[:, :, :, None], ss, NEG_INF).reshape(B, Q_BLOCK, NSA_KV_HEADS, NSA_GROUP, n_sel * SLC_BLOCK)
        p_s = jax.nn.softmax(ss, axis=-1)
        o_s = jnp.einsum('bqkgm,bqkmd->bqkgd', p_s.astype(vs.dtype),
                         vs.reshape(B, Q_BLOCK, NSA_KV_HEADS, n_sel * SLC_BLOCK, HEAD_DIM))
        kw = lax.dynamic_slice_in_dim(k_win_p, s0, WIN + Q_BLOCK, axis=1)
        vw = lax.dynamic_slice_in_dim(v_win_p, s0, WIN + Q_BLOCK, axis=1)
        kpos = s0 - WIN + jnp.arange(WIN + Q_BLOCK, dtype=jnp.int32)
        wmask = (kpos[None, :] <= qpos[:, None]) & (kpos[None, :] > qpos[:, None] - WIN) & (kpos[None, :] >= 0)
        sw = jnp.einsum('bqkgd,bmkd->bqkgm', q_i, kw, preferred_element_type=jnp.float32) * scale
        p_w = jax.nn.softmax(jnp.where(wmask[None, :, None, None, :], sw, NEG_INF), axis=-1)
        o_w = jnp.einsum('bqkgm,bmkd->bqkgd', p_w.astype(vw.dtype), vw)
        g = g_i.astype(o_c.dtype)[..., None]
        return g[:, :, 0] * o_c + g[:, :, 1] * o_s + g[:, :, 2] * o_w

    o = lax.map(block, (q_blocks, g_blocks, starts))
    return o.swapaxes(0, 1).reshape(B, S, qd) @ w_o

def setup_inputs(seed: int = 0) -> dict:
    key = jax.random.key(seed)
    ks = iter(jax.random.split(key, 64))

    def dense(shape, fan_in):
        return jax.random.normal(next(ks), shape, jnp.float32) * fan_in ** -0.5

    def gain():
        return 1.0 + 0.05 * jax.random.normal(next(ks), (D_MODEL,), jnp.float32)

    nsa_in_width = N_HEADS * HEAD_DIM + 6 * NSA_KV_HEADS * HEAD_DIM + 3 * N_HEADS
    return {
        "x": jax.random.normal(next(ks), (BATCH, SEQ, D_MODEL), jnp.float32),
        "positions": jnp.arange(SEQ, dtype=jnp.int32),
        "l0_norm_mix": gain(),
        "l0_fox_w_qkv": dense((D_MODEL, 3 * D_MODEL), D_MODEL),
        "l0_fox_w_f": dense((D_MODEL, N_HEADS), D_MODEL),
        "l0_fox_b_f": 4.0 + 0.5 * jax.random.normal(next(ks), (N_HEADS,), jnp.float32),
        "l0_fox_w_o": dense((D_MODEL, D_MODEL), D_MODEL),
        "l0_norm_mlp": gain(),
        "l0_mlp_w1": dense((D_MODEL, D_FF), D_MODEL),
        "l0_mlp_w2": dense((D_FF, D_MODEL), D_FF),
        "l1_norm_mix": gain(),
        "l1_pool_w": dense((len(POOL_WINDOWS), POOL_GROUP, POOL_GROUP), POOL_GROUP),
        "l1_pool_scale": 1.0 + 0.1 * jax.random.normal(next(ks), (D_MODEL,), jnp.float32),
        "l1_norm_mlp": gain(),
        "l1_mlp_w1": dense((D_MODEL, D_FF), D_MODEL),
        "l1_mlp_w2": dense((D_FF, D_MODEL), D_FF),
        "l2_norm_mix": gain(),
        "l2_conv_w_in": dense((D_MODEL, 3 * D_MODEL), D_MODEL),
        "l2_conv_w": dense((CONV_WIDTH, D_MODEL), CONV_WIDTH),
        "l2_conv_w_out": dense((D_MODEL, D_MODEL), D_MODEL),
        "l2_norm_mlp": gain(),
        "l2_mlp_w1": dense((D_MODEL, D_FF), D_MODEL),
        "l2_mlp_w2": dense((D_FF, D_MODEL), D_FF),
        "l3_norm_mix": gain(),
        "l3_nsa_w_in": dense((D_MODEL, nsa_in_width), D_MODEL),
        "l3_nsa_cmp_pe_k": 0.1 * jax.random.normal(next(ks), (CMP_BLOCK, HEAD_DIM), jnp.float32),
        "l3_nsa_cmp_w1_k": dense((CMP_BLOCK * HEAD_DIM, CMP_HIDDEN), CMP_BLOCK * HEAD_DIM),
        "l3_nsa_cmp_w2_k": dense((CMP_HIDDEN, HEAD_DIM), CMP_HIDDEN),
        "l3_nsa_cmp_pe_v": 0.1 * jax.random.normal(next(ks), (CMP_BLOCK, HEAD_DIM), jnp.float32),
        "l3_nsa_cmp_w1_v": dense((CMP_BLOCK * HEAD_DIM, CMP_HIDDEN), CMP_BLOCK * HEAD_DIM),
        "l3_nsa_cmp_w2_v": dense((CMP_HIDDEN, HEAD_DIM), CMP_HIDDEN),
        "l3_nsa_w_o": dense((N_HEADS * HEAD_DIM, D_MODEL), N_HEADS * HEAD_DIM),
        "l3_norm_mlp": gain(),
        "l3_mlp_w1": dense((D_MODEL, D_FF), D_MODEL),
        "l3_mlp_w2": dense((D_FF, D_MODEL), D_FF),
        "final_norm": gain(),
    }

def reference(x, positions,
              l0_norm_mix, l0_fox_w_qkv, l0_fox_w_f, l0_fox_b_f, l0_fox_w_o, l0_norm_mlp, l0_mlp_w1, l0_mlp_w2,
              l1_norm_mix, l1_pool_w, l1_pool_scale, l1_norm_mlp, l1_mlp_w1, l1_mlp_w2,
              l2_norm_mix, l2_conv_w_in, l2_conv_w, l2_conv_w_out, l2_norm_mlp, l2_mlp_w1, l2_mlp_w2,
              l3_norm_mix, l3_nsa_w_in, l3_nsa_cmp_pe_k, l3_nsa_cmp_w1_k, l3_nsa_cmp_w2_k,
              l3_nsa_cmp_pe_v, l3_nsa_cmp_w1_v, l3_nsa_cmp_w2_v, l3_nsa_w_o, l3_norm_mlp, l3_mlp_w1, l3_mlp_w2,
              final_norm):
    cos, sin = rope_tables(positions)
    mixers = (
        lambda t: fox_attention(t, l0_fox_w_qkv, l0_fox_w_f, l0_fox_b_f, l0_fox_w_o),
        lambda t: pool_mixer(t, l1_pool_w, l1_pool_scale),
        lambda t: short_conv_mixer(t, l2_conv_w_in, l2_conv_w, l2_conv_w_out),
        lambda t: nsa_attention(t, cos, sin, l3_nsa_w_in, l3_nsa_cmp_pe_k, l3_nsa_cmp_w1_k, l3_nsa_cmp_w2_k,
                                l3_nsa_cmp_pe_v, l3_nsa_cmp_w1_v, l3_nsa_cmp_w2_v, l3_nsa_w_o),
    )
    norm_mix = (l0_norm_mix, l1_norm_mix, l2_norm_mix, l3_norm_mix)
    norm_mlp = (l0_norm_mlp, l1_norm_mlp, l2_norm_mlp, l3_norm_mlp)
    mlp_w1 = (l0_mlp_w1, l1_mlp_w1, l2_mlp_w1, l3_mlp_w1)
    mlp_w2 = (l0_mlp_w2, l1_mlp_w2, l2_mlp_w2, l3_mlp_w2)
    h = x
    for i in range(DEPTH):
        h = h + mixers[i % N_MIXERS](rmsnorm(h, norm_mix[i]))
        h = h + sq_relu_mlp(rmsnorm(h, norm_mlp[i]), mlp_w1[i], mlp_w2[i])
    return rmsnorm(h, final_norm)


_drawn_inputs = setup_inputs


def setup_inputs(seed=0):
    import zlib

    import numpy as np

    out = dict(_drawn_inputs(seed))
    spreads = {}
    factors = {'l0_norm_mix': 2.669, 'l1_norm_mix': 3.744, 'l1_norm_mlp': 3.543}
    for name, (base, spread) in spreads.items():
        noise = np.random.default_rng([zlib.crc32(name.encode()), seed]).standard_normal(out[name].shape)
        drawn = base * np.exp(spread * noise) if base else spread * noise
        out[name] = __import__('jax').numpy.asarray(drawn.astype(out[name].dtype))
    for name, factor in factors.items():
        out[name] = (out[name] * factor).astype(out[name].dtype)
    return out
```

```python
from contextlib import ExitStack

import numpy as np

import concourse.bass as bass
from concourse import mybir

F32 = mybir.dt.float32
F32R = mybir.dt.float32r
ACT = mybir.ActivationFunctionType
ALU = mybir.AluOpType

T = 1024
D = 1024
P = 128
NT = T // P
KD = D // P
HALF = 512
HEADS = 16
HD = 64
PAIRS = HEADS // 2
FF = 4096
CHUNK = 512
FT = CHUNK // P
CHUNKS = FF // CHUNK
SCALE = HD ** -0.5
EPS = 1e-6
NEG = -1e30
WINDOWS = (2, 4, 8, 16)
HALO = max(WINDOWS)
KB = 1024
ARENA = 206 * KB
HEAD_LOADS = 8
BAND = len(WINDOWS) * (2 * P + HALO)

U_V0, U_F, U_V1, U_QK, U_O0, U_O1 = 0, 4, 5, 9, 25, 29
U_MLP = (35, 101)
U_POOL = 97
UP_QK, UP_MLP, UP_ALL = 0, (32, 96), 160
DN_V0, DN_V1, DN_O, DN_MLP, DN_POOL = 0, 8, 16, (32, 176), 160
TR_IN, TR_O, TR_POOL, TR_MLP1 = 0, 8, 24, 32


def o_phase_order():
    order = [("attn", 0)]
    for t in range(NT):
        if t + 1 < NT:
            order.append(("attn", t + 1))
        if t >= 1:
            order.append(("norm", t - 1))
    return order + [("norm", NT - 1)]


O_ORDER = {key: TR_O + n for n, key in enumerate(o_phase_order())}


def up_bank(g):
    return g % 4


def wide_tile(p, s):
    q = s % 16
    return 8 * p + (8 * (s // 16) + 4 * (q // 8) + (q % 8 - 4))


def host_constants():
    ident = np.eye(P, dtype=np.float32)
    row, col = np.arange(P)[:, None], np.arange(P)[None, :]
    mask = np.where(col > row, np.float32(NEG), np.float32(0))
    later, first, halo = [], [], []
    for w in WINDOWS:
        inside = (col - row >= 0) & (col - row < w)
        later.append(inside / w - ident)
        first.append(inside / np.minimum(col + 1, w) - ident)
        halo.append((np.arange(HALO)[None, :] + P - row < w) / w)
    band = np.concatenate([np.concatenate(m, 1) for m in (later, first, halo)], 1)
    return (np.concatenate([ident, mask], 1).astype(np.float32), band.astype(np.float32))


def build(nc, x, norm0, w_qkv, w_f, b_f, w_o, norm1, w1_0, w2_0, norm2, w_pool, pool_scale, norm3,
          w1_1, w2_1, norm4, const, band_in, out):
    gains = (norm0, norm1, norm2, norm3, norm4)
    w1s, w2s = (w1_0, w1_1), (w2_0, w2_1)
    ctx = ExitStack()
    with ctx:
        def sem(name):
            return ctx.enter_context(nc.semaphore(name))

        base = (nc.sbuf_base + 31) // 32 * 32
        ctx.enter_context(nc.sbuf_tensor("arena", [P, ARENA // 4], F32))

        def at(name, shape, dt, off):
            return nc.alloc_sbuf_tensor_at(name, shape, dt, offset=base + off)

        class Parts:
            def __init__(self, name, cols, off):
                self.hi = at(name + "_hi", [P, cols], F32R, off)
                self.lo = at(name + "_lo", [P, cols], F32R, off + 4 * cols)

        A, B, C, DD, E, FF_, G = (n * KB for n in (0, 32, 96, 128, 144, 176, 184))
        x_sb = at("x_res", [P, NT * D], F32, A)
        v1_w = [Parts(f"wv1_{j}", 1024, A + 8 * KB * j) for j in range(4)]
        q_tmp = Parts("q_tmp", T, A)
        k_tmp = Parts("k_tmp", T, A + 8 * KB)
        o_sb = at("attn_out", [P, NT * D], F32, A)
        hT = Parts("hT", KD * T, B)
        p_ring = [at(f"probs{i}", [P, T], F32, B + 4 * KB * i) for i in range(4)]
        pt_a = [at(f"probsT_a{i}", [P, HALF], F32, B + 16 * KB + 2 * KB * i) for i in range(2)]
        pt_b = [at(f"probsT_b{i}", [P, HALF], F32, B + 20 * KB + 2 * KB * i) for i in range(2)]
        v_sb = at("values", [P, NT * D], F32, C)
        h1 = Parts("hidden", FT * T, C)
        wo1 = [Parts(f"wo1_{j}", 1024, C + 8 * KB * j) for j in range(4)]
        w_slot = [Parts(f"wslot{i}", 1024, DD + 8 * KB * i) for i in range(2)]
        mask_f32 = at("mask_f32", [P, P], F32, DD)
        y_ring = [at(f"y{i}", [P, D], F32, DD + 4 * KB * i) for i in range(2)]
        wide = [Parts(f"wide{j}", 1024, E + 8 * KB * j) for j in range(4)]
        qs = [at(f"q_stack{i}", [P, T], F32R, E + 16 * KB * i) for i in range(2)]
        kh2 = [at(f"k_hi2_{i}", [P, T], F32R, E + 16 * KB * i + 4 * KB) for i in range(2)]
        kl2 = [at(f"k_lo2_{i}", [P, T], F32R, E + 16 * KB * i + 8 * KB) for i in range(2)]
        decay = [at(f"decay{i}", [P, T], F32, E + 16 * KB * i + 12 * KB) for i in range(2)]
        stage = [at(f"stage{i}", [P, 1024], F32, FF_ + 4 * KB * i) for i in range(2)]
        xn = [at(f"xn{i}", [P, D], F32, G + 4 * KB * i) for i in range(2)]
        gain_sb = at("gain", [P, D], F32, G + 8 * KB)
        pscale_sb = at("pool_scale", [P, D], F32, G + 12 * KB)
        ident = at("ident", [P, P], F32, G + 16 * KB)
        ident_r = at("ident_r", [P, P], F32R, G + 16 * KB + 512)
        mask_r = at("mask_r", [P, P], F32R, G + 17 * KB)
        band = at("band", [P, BAND], F32, G + 17 * KB + 512)
        v_head = [at(f"v_head{i}", [P, NT * HD], F32, G + 17 * KB + 512 + 2 * KB * i) for i in range(2)]
        small = at("small", [P, 64], F32, G + 21 * KB + 768)
        ss, ms, rt, rs = (small[:, i:i + 1] for i in range(4))
        bf_sb = small[0:HEADS, 4:5]
        mx, negmx, rsum, rinv = (small[:, 8 + 8 * i:16 + 8 * i] for i in range(4))

        ps = ctx.enter_context(nc.psum_tensor("acc", [P, 8 * HALF], F32))

        def bank(b, n=1):
            return ps[:, b * HALF:(b + n) * HALF]

        q_parts = nc.dram_tensor("q_parts", [2, D, T], F32, kind="Internal").ap()
        k_parts = nc.dram_tensor("k_parts", [2, D, T], F32, kind="Internal").ap()
        cum_dram = nc.dram_tensor("cum_decay", [HEADS, T], F32, kind="Internal").ap()

        const_in = sem("const_in")
        mask_in = sem("mask_in")
        bf_in = sem("bf_in")
        gain_in = sem("gain_in")
        band_in_s = sem("band_loaded")
        pscale_in = sem("pscale_in")
        x_in = [sem(f"x_in{t}") for t in range(NT)]
        stage_in = [sem(f"stage_in{i}") for i in range(2)]
        head_in = [sem(f"head_in{i}") for i in range(2)]
        consts_ready = sem("consts_ready")
        stage_zeroed = sem("stage_zeroed")
        w_hi, w_lo = sem("w_hi"), sem("w_lo")
        sq_done, ms_done, rt_done, rs_done, xn_done = (sem(n) for n in ("sq_done", "ms_done", "rt_done", "rs_done", "xn_done"))
        tr_full, tr_hi, tr_lo = sem("tr_full"), sem("tr_hi"), sem("tr_lo")
        gate_full = sem("gate_full")
        up_full, up_act, up_hi, up_lo = sem("up_full"), sem("up_act"), sem("up_hi"), sem("up_lo")
        dn_full, dn_mul, dn_used = sem("dn_full"), sem("dn_mul"), sem("dn_used")
        gate_act, gate_dve, gate_stored = sem("gate_act"), sem("gate_dve"), sem("gate_stored")
        q_stored, k_stored = sem("q_stored"), sem("k_stored")
        qk_last_stored = sem("qk_last_stored")
        s_full, bias_done, negmx_done, p_done = sem("s_full"), sem("bias_done"), sem("negmx_done"), sem("p_done")
        ta_full, tb_full, pta_done, ptb_done = sem("ta_full"), sem("tb_full"), sem("pta_done"), sem("ptb_done")
        o_full, rinv_done, o_done = sem("o_full"), sem("rinv_done"), sem("o_done")
        y_out = [sem(f"y_out{i}") for i in range(2)]

        block = ctx.enter_context(nc.Block())

        def unit_dst(u):
            if u < U_F:
                return wide[u - U_V0]
            if u == U_F:
                return w_slot[0]
            if u < U_QK:
                return v1_w[u - U_V1]
            if u < U_O0:
                return w_slot[(u - U_QK + 1) % 2]
            if u < U_O1:
                return (w_slot + wide[2:])[u - U_O0]
            if u < U_MLP[0] - 2:
                return wo1[u - U_O1]
            if u < U_MLP[0]:
                return w_slot[u - (U_MLP[0] - 2)]
            if u < U_POOL + 2:
                return wide[u - U_POOL]
            return w_slot[u - (U_MLP[1] - 2)]

        wo0 = w_slot + wide[2:]

        def three_passes(pe, dst, pairs):
            n = 0
            for (s_hi, s_lo), (m_hi, m_lo) in pairs:
                for s, m in ((s_lo, m_hi), (s_hi, m_lo), (s_hi, m_hi)):
                    mm = pe.matmul(dst, s, m, start=(n == 0), stop=(n == 3 * len(pairs) - 1))
                    n += 1
            return mm

        @block.sync
        def _(sp):
            def load_unit(u, parity, src, cols=None):
                if not isinstance(u, int) or u >= 2:
                    sp.wait_ge(w_lo, u - 1)
                dst = stage[parity][:, :] if cols is None else stage[parity][:, :].rearrange("p (k n) -> p k n", n=cols)
                sp.dma_start(dst, src).then_inc(stage_in[parity], 16)

            w_cols = lambda w, c0, n: w.rearrange("(k p) n -> p k n", p=P)[:, :, bass.ds(c0, n)]

            def load_wide(first, w, c0):
                for j in range(4):
                    load_unit(first + j, (first + j) % 2, w_cols(w, c0, HALF)[:, 2 * j:2 * j + 2, :], HALF)

            def store_parts(tmp, dram, p, ready, stored):
                sp.wait_ge(up_lo, ready)
                for part, t in enumerate((tmp.hi, tmp.lo)):
                    sp.dma_start(dram[part, bass.ds(p * P, P), :], t[:, :].bitcast(F32)).then_inc(stored, 16)

            def qk_pair(p, last=False, first=False):
                if not last:
                    load_unit(U_QK + 2 + 2 * p, (U_QK + 2) % 2, w_cols(w_qkv, p * P + P, P), P)
                    load_unit(U_QK + 3 + 2 * p, (U_QK + 3) % 2, w_cols(w_qkv, p * P + (D + P), P), P)
                store_parts(q_tmp, q_parts, p, UP_QK + 4 * p + 2, qk_last_stored if last else q_stored)
                store_parts(k_tmp, k_parts, p, UP_QK + 4 * p + 4, qk_last_stored if last else k_stored)

            def load_head(h, slot):
                s = head_in[slot]
                for half in range(2):
                    rows = slice(half * HD, (half + 1) * HD)
                    for dst, src in ((qs, q_parts[half]), (kh2, k_parts[0]), (kl2, k_parts[1])):
                        sp.dma_start(dst[slot][rows, :].bitcast(F32), src[bass.ds(h * HD, HD), :]).then_inc(s, 16)
                sp.dma_start(decay[slot][:, :], cum_dram[bass.ds(h, 1), :].to_broadcast([P, T])).then_inc(s, 16)
                sp.dma_start(v_head[slot][:, :].rearrange("p (k d) -> p k d", d=HD),
                             v_sb[:, :].rearrange("p (k c) -> p k c", c=D)[:, :, bass.ds(h * HD, HD)]).then_inc(s, 16)

            load_wide(U_V0, w_qkv, 2 * D)
            sp.wait_ge(stage_zeroed, 1)
            sp.dma_start(stage[0][:, :].rearrange("p (k n) -> p k n", n=P)[:, :, 0:HEADS],
                         w_f.rearrange("(k p) n -> p k n", p=P)).then_inc(stage_in[0], 16)
            load_wide(U_V1, w_qkv, 2 * D + HALF)
            load_unit(U_QK, U_QK % 2, w_cols(w_qkv, 0, P), P)
            load_unit(U_QK + 1, (U_QK + 1) % 2, w_cols(w_qkv, D, P), P)
            sp.wait_ge(gate_dve, 3)
            sp.dma_start(cum_dram[:, :], xn[0][0:HEADS, :]).then_inc(gate_stored, 16)
            qk_pair(0)
            with sp.Fori(1, PAIRS - 1) as p:
                qk_pair(p)
            load_unit(U_O0, U_O0 % 2, w_cols(w_o, 0, HALF)[:, 0:2, :], HALF)
            sp.wait_ge(q_stored, 32 * (PAIRS - 1))
            sp.wait_ge(k_stored, 32 * (PAIRS - 1))
            sp.wait_ge(gate_stored, 16)
            sp.wait_ge(dn_used, DN_O)
            load_head(0, 0)
            load_head(1, 1)
            qk_pair(PAIRS - 1, last=True)
            for j in range(1, 4):
                load_unit(U_O0 + j, (U_O0 + j) % 2, w_cols(w_o, 0, HALF)[:, 2 * j:2 * j + 2, :], HALF)
            sp.wait_ge(qk_last_stored, 64)
            with sp.Fori(1, PAIRS) as p:
                for s in range(2):
                    sp.wait_ge(o_full, 16 * p + (8 * s - 8))
                    load_head(2 * p + s, s)
            for j in range(4):
                load_unit(U_O1 + j, (U_O1 + j) % 2, w_cols(w_o, HALF, HALF)[:, 2 * j:2 * j + 2, :], HALF)

            def load_w1(u, parity, w, c, f):
                load_unit(u, parity, w_cols(w, c * CHUNK + f * P, P), P)

            def load_w2(u, parity, w, c, f):
                load_unit(u, parity, w[bass.ds(c * CHUNK + f * P, P), :])

            def mlp_units(layer, c, last=False):
                u0, w1, w2 = U_MLP[layer], w1s[layer], w2s[layer]
                plan = [("w2", 0, 0), ("w1", 0, 2), ("w2", 0, 1), ("w1", 0, 3), ("w2", 0, 2)]
                plan += [("w2", 0, 3)] if last else [("w1", 1, 0), ("w2", 0, 3), ("w1", 1, 1)]
                for j, (kind, ahead, f) in enumerate(plan):
                    (load_w1 if kind == "w1" else load_w2)(u0 + 8 * c + j, (u0 + j) % 2, w1 if kind == "w1" else w2, c + ahead, f)

            for layer in range(2):
                u0 = U_MLP[layer]
                if layer:
                    for j in range(2):
                        load_unit(U_POOL + j, (U_POOL + j) % 2,
                                  w_pool.rearrange("g (k p) o -> k p g o", p=P)[j], 2 * P)
                load_w1(u0 - 2, (u0 - 2) % 2, w1s[layer], 0, 0)
                load_w1(u0 - 1, (u0 - 1) % 2, w1s[layer], 0, 1)
                with sp.Fori(0, CHUNKS - 1) as c:
                    mlp_units(layer, c)
                mlp_units(layer, CHUNKS - 1, last=True)
            for t in range(NT):
                sp.wait_ge(xn_done, 4 * NT + t + 1)
                sp.dma_start(out[0, t * P:(t + 1) * P, :], y_ring[t % 2][:, :]).then_inc(y_out[t % 2], 16)
            for s in y_out:
                sp.wait_ge(s, 16 * NT // 2)

        @block.gpsimd
        def _(gp):
            def load_gain(n):
                gp.dma_start(gain_sb[:, :], gains[n].rearrange("(a n) -> a n", a=1).to_broadcast([P, D])).then_inc(gain_in, 16)

            def load_x(t):
                gp.dma_start(x_sb[:, t * D:(t + 1) * D], x[0, t * P:(t + 1) * P, :]).then_inc(x_in[t], 16)

            for t in range(2):
                load_x(t)
            load_gain(0)
            gp.dma_start(ident[:, :], const[:, 0:P]).then_inc(const_in, 16)
            for t in range(2, NT):
                load_x(t)
            gp.dma_start(mask_f32[:, :], const[:, P:2 * P]).then_inc(mask_in, 16)
            gp.dma_start(bf_sb, b_f.rearrange("(a n) -> a n", n=1)).then_inc(bf_in, 16)
            gp.wait_ge(w_lo, U_F - 1)
            gp.memset(stage[0][:, :], 0.0).then_inc(stage_zeroed, 1)
            gp.wait_ge(gate_dve, 3)
            load_gain(1)
            gp.dma_start(pscale_sb[:, :], pool_scale.rearrange("(a n) -> a n", a=1).to_broadcast([P, D])).then_inc(pscale_in, 16)
            for t in range(NT):
                gp.wait_ge(tr_full, O_ORDER["attn", t] + 1)
                load_x(t)
            gp.dma_start(band[:, :], band_in).then_inc(band_in_s, 16)
            for n in (2, 3, 4):
                gp.wait_ge(xn_done, NT * n)
                load_gain(n)

        @block.scalar
        def _(act):
            def split(u, parity, dst):
                act.wait_ge(stage_in[parity], 16 * (u // 2 + 1) if isinstance(u, int) else u)
                act.activation(dst.hi[:, :], stage[parity][:, :], ACT.Copy).then_inc(w_hi, 1)

            def split_static(u):
                split(u, u % 2, unit_dst(u))

            def norm_tile(n, t, ready=None, buf=None, buf_free=()):
                if ready is not None:
                    act.wait_ge(*ready)
                for w in buf_free:
                    act.wait_ge(*w)
                act.activation(buf[:, :], x_sb[:, t * D:(t + 1) * D], ACT.Square, accum_out=ss).then_inc(sq_done, 1)
                act.wait_ge(ms_done, n * NT + t + 1)
                act.activation(rt, ms, ACT.Sqrt).then_inc(rt_done, 1)

            def tr_evac(i, t, dst):
                act.wait_ge(tr_full, i + 1)
                for b in range(2):
                    act.activation(dst.hi[:, :].rearrange("p (k n) -> p k n", n=T)[:, 4 * b:4 * b + 4, t * P:(t + 1) * P],
                                   bank(2 * (i % 2) + b).rearrange("p (k n) -> p k n", n=P), ACT.Copy).then_inc(tr_hi, 1)

            def v_evac(g):
                half, t = divmod(g, NT)
                act.wait_ge(dn_full, g + 1)
                act.activation(v_sb[:, t * D + half * HALF:t * D + (half + 1) * HALF], bank(4 + g % 4), ACT.Copy).then_inc(dn_used, 1)

            for u in range(U_V0, U_V0 + 4):
                split_static(u)
            for t in range(NT):
                norm_tile(0, t, (x_in[t], 16), xn[0], [(tr_full, t)] if t else [])
                if t >= 1:
                    tr_evac(TR_IN + t - 1, t - 1, hT)
                if t >= 2:
                    v_evac(t - 2)
            tr_evac(TR_IN + 7, 7, hT)
            act.wait_ge(mask_in, 16)
            act.wait_ge(const_in, 16)
            act.activation(mask_r[:, :], mask_f32[:, :], ACT.Copy).then_inc(consts_ready, 1)
            act.activation(ident_r[:, :], ident[:, :], ACT.Copy).then_inc(consts_ready, 1)
            act.wait_ge(consts_ready, 2)
            split_static(U_F)
            v_evac(6)
            v_evac(7)
            act.wait_ge(xn_done, NT)
            for u in range(U_V1, U_V1 + 4):
                split_static(u)
            split_static(U_QK)
            gate_ps = bank(2, 2)[0:HEADS, :]
            act.wait_ge(bf_in, 16)
            act.wait_ge(gate_full, 2)
            act.activation(xn[0][0:HEADS, :], gate_ps, ACT.Abs, bias=bf_sb).then_inc(gate_act, 1)
            act.wait_ge(gate_act, 1)
            act.activation(xn[0][0:HEADS, :], xn[0][0:HEADS, :], ACT.Exp, scale=-1.0).then_inc(gate_act, 1)
            act.wait_ge(gate_act, 2)
            act.activation(xn[0][0:HEADS, :], xn[0][0:HEADS, :], ACT.Ln, bias=1.0).then_inc(gate_act, 1)
            split_static(U_QK + 1)
            for t in range(NT):
                v_evac(DN_V1 + t)

            def qk_pair(p, first=False, last=False):
                for j in range(4):
                    tmp, half = (q_tmp, k_tmp)[j // 2], j % 2
                    if not first and half == 0:
                        act.wait_ge((q_stored, k_stored)[j // 2], 32 * p)
                    act.wait_ge(up_full, UP_QK + 4 * p + j + 1)
                    act.activation(tmp.hi[:, half * HALF:(half + 1) * HALF], bank(up_bank(UP_QK + j)), ACT.Copy).then_inc(up_hi, 1)
                    if half == 1 and not last:
                        u = U_QK + 2 + j // 2
                        act.wait_ge(stage_in[u % 2], 16 * p + 16 * (u // 2 + 1))
                        act.activation(w_slot[(u - U_QK + 1) % 2].hi[:, :], stage[u % 2][:, :], ACT.Copy).then_inc(w_hi, 1)

            qk_pair(0, first=True)
            with act.Fori(1, PAIRS - 1) as p:
                qk_pair(p)
            qk_pair(PAIRS - 1, last=True)
            split_static(U_O0)
            split_static(U_O0 + 1)

            def exp_tile(p, s, first):
                j, w = 16 * p + s, (s % 8 + 1) * P
                act.wait_ge(negmx_done, j + 1)
                if not first or s >= 4:
                    if (s - 4) % 8 < 4:
                        act.wait_ge(ta_full, j - 3)
                    else:
                        act.wait_ge(tb_full, wide_tile(p, s - 4) + 1)
                if not first or s >= 8:
                    act.wait_ge(o_done, j - 7)
                act.activation(p_ring[s % 4][:, 0:w], bank(2 * (s % 2), 2)[:, 0:w], ACT.Exp,
                               bias=negmx[:, s % 8:s % 8 + 1], scale=SCALE,
                               accum_out=rsum[:, s % 8:s % 8 + 1]).then_inc(p_done, 1)

            def evac_a(p, s, first=False):
                j, w = 16 * p + s, min(s % 8 + 1, 4) * P
                act.wait_ge(ta_full, j + 1)
                if not first or s >= 2:
                    act.wait_ge(o_full, j - 1)
                act.activation(pt_a[s % 2][:, 0:w], bank(4)[:, 0:w], ACT.Copy).then_inc(pta_done, 1)

            def attention(p, first=False):
                for s in range(16):
                    exp_tile(p, s, first)
                    if not first or s >= 2:
                        evac_a(p, s - 2, first)

            attention(0, first=True)
            with act.Fori(1, PAIRS) as p:
                attention(p)
            for s in (14, 15):
                evac_a(PAIRS - 1, s)

            for u in (U_O0 + 2, U_O0 + 3):
                split_static(u)
            tr_evac(O_ORDER["attn", 0], 0, hT)
            for u in range(U_O1, U_O1 + 4):
                split_static(u)
            for t in range(NT):
                if t + 1 < NT:
                    tr_evac(O_ORDER["attn", t + 1], t + 1, hT)
                if t == NT - 1:
                    act.wait_ge(dn_full, DN_O + 16)
                    split_static(U_MLP[0] - 2)
                    split_static(U_MLP[0] - 1)
                norm_tile(1, t, (dn_used, DN_O + 2 * t + 2), xn[0],
                          [(tr_full, O_ORDER["norm", t - 1] + 1)] if t else [(gate_stored, 16)])
                if t >= 1:
                    tr_evac(O_ORDER["norm", t - 1], t - 1, hT)
            tr_evac(O_ORDER["norm", 7], 7, hT)

            def mlp_up(layer, c, last=False):
                g0, u0 = UP_MLP[layer], U_MLP[layer]
                plan = [(0, wide[0]), (1, w_slot[0]), (2, wide[1]), (3, w_slot[1]), (4, wide[2])]
                plan += [(5, wide[3]), None, None] if last else [(5, w_slot[0]), (6, wide[3]), (7, w_slot[1])]
                for j in range(8):
                    f, half = divmod(j, 2)
                    b = bank(up_bank(g0 + j))
                    g = g0 + 8 * c + j
                    act.wait_ge(up_full, g + 1)
                    act.activation(b, b, ACT.Relu).then_inc(up_act, 1)
                    act.wait_ge(up_act, 2 * (g - UP_MLP[0]) + 1)
                    act.activation(b, b, ACT.Square).then_inc(up_act, 1)
                    act.wait_ge(up_act, 2 * (g - UP_MLP[0]) + 2)
                    act.activation(h1.hi[:, f * T + half * HALF:f * T + (half + 1) * HALF], b, ACT.Copy).then_inc(up_hi, 1)
                    if plan[j]:
                        n, dst = plan[j]
                        act.wait_ge(stage_in[(u0 + n) % 2], 64 * c + 16 * ((u0 + n) // 2 + 1))
                        act.activation(dst.hi[:, :], stage[(u0 + n) % 2][:, :], ACT.Copy).then_inc(w_hi, 1)

            for layer in range(2):
                with act.Fori(0, CHUNKS - 1) as c:
                    mlp_up(layer, c)
                mlp_up(layer, CHUNKS - 1, last=True)
                dn0 = DN_MLP[layer] + 16 * (CHUNKS - 1)
                if layer == 0:
                    for t in range(NT):
                        norm_tile(2, t, (dn_used, dn0 + 2 * t + 2), xn[t % 2], [(tr_full, TR_POOL + t)])
                        if t >= 1:
                            tr_evac(TR_POOL + t - 1, t - 1, hT)
                    act.wait_ge(dn_full, dn0 + 16)
                    split_static(U_POOL)
                    split_static(U_POOL + 1)
                    tr_evac(TR_POOL + 7, 7, hT)
                    split_static(U_MLP[1] - 2)
                    split_static(U_MLP[1] - 1)
                    for t in range(NT):
                        norm_tile(3, t, (dn_used, DN_POOL + 2 * t + 2), xn[0],
                                  [(tr_full, TR_MLP1 + t)])
                        if t >= 1:
                            tr_evac(TR_MLP1 + t - 1, t - 1, hT)
                    tr_evac(TR_MLP1 + 7, 7, hT)
                else:
                    for t in range(NT):
                        norm_tile(4, t, (dn_used, dn0 + 2 * t + 2), y_ring[t % 2],
                                  [(y_out[t % 2], 16 * (t // 2))] if t >= 2 else [])

        @block.vector
        def _(dve):
            def split(u_next, parity, dst):
                dve.wait_ge(w_hi, u_next)
                dve.tensor_tensor(dst.lo[:, :], stage[parity][:, :], dst.hi[:, :].bitcast(F32), ALU.subtract).then_inc(w_lo, 1)

            def split_static(u):
                split(u + 1, u % 2, unit_dst(u))

            def norm_tile(n, t, dst, dst_free=()):
                i = n * NT + t + 1
                dve.wait_ge(sq_done, i)
                dve.tensor_scalar(ms, ss, 1.0 / D, EPS, ALU.mult, ALU.add).then_inc(ms_done, 1)
                dve.wait_ge(rt_done, i)
                if i > 1:
                    dve.wait_ge(xn_done, i - 1)
                dve.reciprocal(rs, rt).then_inc(rs_done, 1)
                dve.wait_ge(rs_done, i)
                if t == 0:
                    dve.wait_ge(gain_in, 16 * (n + 1))
                dve.scalar_tensor_tensor(dst[:, :], x_sb[:, t * D:(t + 1) * D], rs, gain_sb[:, :],
                                         ALU.mult, ALU.mult).then_inc(xn_done, 1)

            def tr_evac(i, t, dst):
                for b in range(2):
                    dve.wait_ge(tr_hi, 2 * i + b + 1)
                    cols = lambda a: a[:, :].rearrange("p (k n) -> p k n", n=T)[:, 4 * b:4 * b + 4, t * P:(t + 1) * P]
                    dve.tensor_tensor(cols(dst.lo), bank(2 * (i % 2) + b).rearrange("p (k n) -> p k n", n=P),
                                      cols(dst.hi).bitcast(F32), ALU.subtract).then_inc(tr_lo, 1)

            def up_evac(g, j, hi, lo):
                dve.wait_ge(up_hi, g + 1)
                dve.tensor_tensor(lo, bank(up_bank(j)), hi.bitcast(F32), ALU.subtract).then_inc(up_lo, 1)

            def add_group(g, j):
                t, half = divmod(j, 2)
                xs = x_sb[:, t * D + half * HALF:t * D + (half + 1) * HALF]
                dve.wait_ge(dn_full, g + 1)
                dve.wait_ge(dn_used, g - 15)
                dve.tensor_tensor(xs, bank(4 + j % 4), xs, ALU.add).then_inc(dn_used, 1)

            for u in range(U_V0, U_V0 + 4):
                split_static(u)
            for t in range(NT):
                norm_tile(0, t, xn[0])
                if t >= 1:
                    tr_evac(TR_IN + t - 1, t - 1, hT)
            tr_evac(TR_IN + 7, 7, hT)
            for u in range(U_F, U_QK + 1):
                split_static(u)
            gate_ps = bank(2, 2)[0:HEADS, :]
            dve.wait_ge(gate_act, 1)
            dve.tensor_scalar(gain_sb[0:HEADS, :], gate_ps, bf_sb, 0.0, ALU.add, ALU.min).then_inc(gate_dve, 1)
            dve.wait_ge(gate_act, 3)
            dve.wait_ge(gate_dve, 1)
            dve.tensor_tensor_scan(gate_ps, gain_sb[0:HEADS, :], xn[0][0:HEADS, :], 0.0, ALU.add, ALU.subtract).then_inc(gate_dve, 1)
            dve.wait_ge(gate_dve, 2)
            dve.tensor_scalar(xn[0][0:HEADS, :], gate_ps, -1.0 / SCALE, None, ALU.mult).then_inc(gate_dve, 1)
            split_static(U_QK + 1)

            def qk_pair(p, last=False):
                for j in range(4):
                    tmp, half = (q_tmp, k_tmp)[j // 2], j % 2
                    cols = slice(half * HALF, (half + 1) * HALF)
                    up_evac(UP_QK + 4 * p + j, UP_QK + j, tmp.hi[:, cols], tmp.lo[:, cols])
                    if half == 1 and not last:
                        u = U_QK + 2 + j // 2
                        split(u + 1 + 2 * p, u % 2, w_slot[(u - U_QK + 1) % 2])

            qk_pair(0)
            with dve.Fori(1, PAIRS - 1) as p:
                qk_pair(p)
            qk_pair(PAIRS - 1, last=True)
            split_static(U_O0)
            split_static(U_O0 + 1)

            def row_sum_inverse(p, s):
                j, q = 16 * p + s, s % 16
                dve.wait_ge(o_full, j + 1)
                dve.reciprocal(rinv[:, q % 8:q % 8 + 1], rsum[:, q % 8:q % 8 + 1]).then_inc(rinv_done, 1)

            def bias_tile(p, s, first):
                j, w = 16 * p + s, (s % 8 + 1) * P
                sc = bank(2 * (s % 2), 2)[:, 0:w]
                if s % 8 == 0:
                    dve.wait_ge(head_in[s // 8], 16 * HEAD_LOADS * p + 16 * HEAD_LOADS)
                dve.wait_ge(s_full, j + 1)
                if not first or s >= 4:
                    row_sum_inverse(p, s - 4)
                dve.tensor_tensor_reduce(out=sc, in0=sc, in1=decay[s // 8][:, 0:w], scale=1.0, scalar=-3.0e38,
                                         op0=ALU.add, op1=ALU.max, accum_out=mx[:, s % 8:s % 8 + 1]).then_inc(bias_done, 1)
                dve.wait_ge(bias_done, j + 1)
                dve.tensor_scalar(negmx[:, s % 8:s % 8 + 1], mx[:, s % 8:s % 8 + 1], -SCALE, None, ALU.mult).then_inc(negmx_done, 1)

            def evac_b(p, s, first=False):
                j, w = 16 * p + s, (s % 8 + 1 - 4) * P
                dve.wait_ge(tb_full, wide_tile(p, s) + 1)
                if not (first and s < 6):
                    dve.wait_ge(o_full, j - 5 if s % 8 < 6 else j - 1)
                dve.tensor_copy(pt_b[s % 2][:, 0:w], bank(5)[:, 0:w]).then_inc(ptb_done, 1)

            def out_tile(p, s):
                j, q = 16 * p + s, s % 16
                dve.wait_ge(rinv_done, j + 1)
                dve.tensor_scalar(o_sb[:, bass.ds(p * P + (s // 16 * P + (q % 8) * D + (q // 8) * HD), HD)],
                                  bank(6 + q % 2)[:, 0:HD], rinv[:, q % 8:q % 8 + 1], None, ALU.mult).then_inc(o_done, 1)

            def attention(p, first=False):
                for s in range(16):
                    bias_tile(p, s, first)
                    if (s - 2) % 8 >= 4 and (not first or s >= 2):
                        evac_b(p, s - 2, first)
                    if not first or s >= 4:
                        out_tile(p, s - 4)

            attention(0, first=True)
            with dve.Fori(1, PAIRS) as p:
                attention(p)
            last = PAIRS - 1
            evac_b(last, 14)
            row_sum_inverse(last, 12)
            out_tile(last, 12)
            evac_b(last, 15)
            for s in (13, 14, 15):
                row_sum_inverse(last, s)
                out_tile(last, s)

            for u in (U_O0 + 2, U_O0 + 3):
                split_static(u)
            tr_evac(O_ORDER["attn", 0], 0, hT)
            for u in range(U_O1, U_O1 + 4):
                split_static(u)
            for t in range(NT):
                if t + 1 < NT:
                    tr_evac(O_ORDER["attn", t + 1], t + 1, hT)
                dve.wait_ge(x_in[t], 32)
                for j in (2 * t, 2 * t + 1):
                    add_group(DN_O + j, j)
                if t == NT - 1:
                    split_static(U_MLP[0] - 2)
                    split_static(U_MLP[0] - 1)
                norm_tile(1, t, xn[0])
                if t >= 1:
                    tr_evac(O_ORDER["norm", t - 1], t - 1, hT)
            tr_evac(O_ORDER["norm", 7], 7, hT)

            def mlp_up(layer, c, last=False):
                g0, u0 = UP_MLP[layer], U_MLP[layer]
                plan = [(0, wide[0]), (1, w_slot[0]), (2, wide[1]), (3, w_slot[1]), (4, wide[2])]
                plan += [(5, wide[3]), None, None] if last else [(5, w_slot[0]), (6, wide[3]), (7, w_slot[1])]
                for j in range(8):
                    f, half = divmod(j, 2)
                    cols = slice(f * T + half * HALF, f * T + (half + 1) * HALF)
                    up_evac(g0 + 8 * c + j, g0 + j, h1.hi[:, cols], h1.lo[:, cols])
                    if plan[j]:
                        n, dst = plan[j]
                        split(u0 + n + 1 + 8 * c, (u0 + n) % 2, dst)

            for layer in range(2):
                with dve.Fori(0, CHUNKS - 1) as c:
                    mlp_up(layer, c)
                    for j in range(16):
                        add_group(DN_MLP[layer] + 16 * c + j, j)
                mlp_up(layer, CHUNKS - 1, last=True)
                dn0 = DN_MLP[layer] + 16 * (CHUNKS - 1)
                for t in range(NT):
                    for j in (2 * t, 2 * t + 1):
                        add_group(dn0 + j, j)
                    if layer == 0:
                        norm_tile(2, t, xn[t % 2])
                        if t >= 1:
                            tr_evac(TR_POOL + t - 1, t - 1, hT)
                    else:
                        norm_tile(4, t, y_ring[t % 2])
                if layer == 0:
                    split_static(U_POOL)
                    split_static(U_POOL + 1)
                    tr_evac(TR_POOL + 7, 7, hT)
                    split_static(U_MLP[1] - 2)
                    split_static(U_MLP[1] - 1)
                    dve.wait_ge(pscale_in, 16)
                    for t in range(NT):
                        for half in range(2):
                            g = DN_POOL + 2 * t + half
                            cols = slice(half * HALF, (half + 1) * HALF)
                            b = bank(4 + g % 4)
                            dve.wait_ge(dn_full, g + 1)
                            dve.tensor_tensor(b, b, pscale_sb[:, cols], ALU.mult).then_inc(dn_mul, 1)
                            dve.wait_ge(dn_mul, 2 * t + half + 1)
                            add_group(g, 2 * t + half)
                        norm_tile(3, t, xn[0])
                        if t >= 1:
                            tr_evac(TR_MLP1 + t - 1, t - 1, hT)
                    tr_evac(TR_MLP1 + 7, 7, hT)

        @block.tensor
        def _(pe):
            hT_parts = lambda k, c0, n: tuple(a[:, k * T + c0:k * T + c0 + n] for a in (hT.hi, hT.lo))

            def tr_start(i, banks_free=()):
                for w in banks_free:
                    pe.wait_ge(*w)
                if i >= 2:
                    pe.wait_ge(tr_lo, 2 * (i - 2) + 2)

            def transpose_tile(i, src, banks_free=()):
                tr_start(i, banks_free)
                for k in range(KD):
                    dst = bank(2 * (i % 2) + k // 4)[:, (k % 4) * P:(k % 4 + 1) * P]
                    mm = pe.transpose(dst, src[:, k * P:(k + 1) * P], ident[:, :])
                mm.then_inc(tr_full, 1)

            def pool_tile(i, t):
                tr_start(i, [(up_lo, UP_MLP[1])] if t < 2 else [])
                for k in range(KD):
                    g = k // 2
                    dst = bank(2 * (i % 2) + k // 4)[:, (k % 4) * P:(k % 4 + 1) * P]
                    m0 = (g if t else len(WINDOWS) + g) * P
                    mm = pe.matmul(dst, xn[t % 2][:, k * P:(k + 1) * P], band[:, m0:m0 + P], start=True, stop=(t == 0))
                    if t:
                        h0 = 2 * len(WINDOWS) * P + g * HALO
                        mm = pe.matmul(dst[:, 0:HALO], xn[(t - 1) % 2][:, k * P:(k + 1) * P], band[:, h0:h0 + HALO],
                                       start=False, stop=True)
                mm.then_inc(tr_full, 1)

            def wide_group(g, t, tiles):
                if g >= 4:
                    pe.wait_ge(dn_used, g - 3)
                pairs = [(hT_parts(k, t * P, P), tuple(a[:, (k % 2) * HALF:(k % 2 + 1) * HALF]
                                                      for a in (tiles[k // 2].hi, tiles[k // 2].lo))) for k in range(KD)]
                three_passes(pe, bank(4 + g % 4), pairs).then_inc(dn_full, 1)

            def up_group(g_static, slot, half, need, full=up_full):
                for w in need:
                    pe.wait_ge(*w)
                pairs = [(tuple(a[:, k * P:(k + 1) * P] for a in (slot.hi, slot.lo)), hT_parts(k, half * HALF, HALF)) for k in range(KD)]
                three_passes(pe, bank(up_bank(g_static)), pairs).then_inc(full, 1)

            pe.wait_ge(const_in, 16)
            for t in range(NT):
                pe.wait_ge(xn_done, t + 1)
                transpose_tile(TR_IN + t, xn[0])
                if t >= 1:
                    pe.wait_ge(w_lo, U_V0 + 4)
                    pe.wait_ge(tr_lo, 2 * t)
                    wide_group(DN_V0 + t - 1, t - 1, wide)
            pe.wait_ge(tr_lo, 2 * NT)
            wide_group(DN_V0 + 7, 7, wide)
            for half in range(2):
                up_group(2 + half, w_slot[0], half, [(w_lo, U_F + 1)], gate_full)
            pe.wait_ge(w_lo, U_V1 + 4)
            for t in range(NT):
                wide_group(DN_V1 + t, t, v1_w)

            def qk_pair(p, first=False):
                for j in range(4):
                    need = [(w_lo, U_QK + 2 * p + j // 2 + 1)]
                    g = UP_QK + 4 * p + j
                    if not first:
                        need.append((up_lo, g - 3))
                    elif j >= 2:
                        need.append((gate_dve, 3))
                    up_group(UP_QK + j, w_slot[(j // 2 + 1) % 2], j % 2, need)

            qk_pair(0, first=True)
            with pe.Fori(1, PAIRS) as p:
                qk_pair(p)

            def scores(j, s, first, head_count):
                i, slot = s % 8, s // 8
                w = (i + 1) * P
                if i == 0:
                    pe.wait_ge(head_in[slot], head_count)
                if not first or s >= 2:
                    pe.wait_ge(p_done, j - 1)
                q = qs[slot][:, i * P:(i + 1) * P]
                for c0 in range(0, w, HALF):
                    n = min(HALF, w - c0)
                    dst = bank(2 * (s % 2), 2)[:, c0:c0 + n]
                    diag = c0 + n == w
                    pe.matmul(dst, q, kl2[slot][:, c0:c0 + n], start=True, stop=False)
                    mm = pe.matmul(dst, q, kh2[slot][:, c0:c0 + n], start=False, stop=not diag)
                    if diag:
                        mm = pe.matmul(dst[:, n - P:n], ident_r[:, :], mask_r[:, :], start=False, stop=True)
                mm.then_inc(s_full, 1)

            def transposes(p, s, first=False):
                j, q = 16 * p + s, s % 16
                i = q % 8
                pe.wait_ge(p_done, j + 1)
                if not first or s >= 1:
                    pe.wait_ge(pta_done, j)
                for kt in range(min(i + 1, 4)):
                    mm = pe.transpose(bank(4)[:, kt * P:(kt + 1) * P], p_ring[q % 4][:, kt * P:(kt + 1) * P], ident[:, :])
                mm.then_inc(ta_full, 1)
                if i >= 4:
                    if not (first and s == 4):
                        pe.wait_ge(ptb_done, wide_tile(p, s))
                    for kt in range(4, i + 1):
                        mm = pe.transpose(bank(5)[:, (kt - 4) * P:(kt - 3) * P], p_ring[q % 4][:, kt * P:(kt + 1) * P], ident[:, :])
                    mm.then_inc(tb_full, 1)

            def weighted_values(p, s, first=False):
                j, q = 16 * p + s, s % 16
                i, slot = q % 8, q // 8
                pe.wait_ge(pta_done, j + 1)
                if i >= 4:
                    pe.wait_ge(ptb_done, wide_tile(p, s) + 1)
                if not first or s >= 2:
                    pe.wait_ge(o_done, j - 1)
                for kt in range(i + 1):
                    src = (pt_a if kt < 4 else pt_b)[q % 2][:, (kt % 4) * P:(kt % 4 + 1) * P]
                    mm = pe.matmul(bank(6 + q % 2)[:, 0:HD], src, v_head[slot][:, kt * HD:(kt + 1) * HD],
                                   start=(kt == 0), stop=(kt == i))
                mm.then_inc(o_full, 1)

            def attention(p, first=False):
                for s in range(16):
                    scores(16 * p + s, s, first, 16 * HEAD_LOADS * p + 16 * HEAD_LOADS)
                    if not first or s >= 2:
                        transposes(p, s - 2, first)
                    if not first or s >= 3:
                        weighted_values(p, s - 3, first)

            pe.wait_ge(consts_ready, 2)
            pe.wait_ge(up_lo, UP_MLP[0])
            pe.wait_ge(dn_used, DN_O)
            attention(0, first=True)
            with pe.Fori(1, PAIRS) as p:
                attention(p)
            last = PAIRS - 1
            transposes(last, 14)
            weighted_values(last, 13)
            transposes(last, 15)
            weighted_values(last, 14)
            weighted_values(last, 15)

            def attn_tile(t):
                transpose_tile(O_ORDER["attn", t], o_sb[:, t * D:(t + 1) * D], [(o_done, 8 * HEADS)])

            attn_tile(0)
            for t in range(NT):
                if t + 1 < NT:
                    attn_tile(t + 1)
                pe.wait_ge(tr_lo, 2 * O_ORDER["attn", t] + 2)
                pe.wait_ge(w_lo, U_O0 + 4)
                wide_group(DN_O + 2 * t, t, wo0)
                pe.wait_ge(w_lo, U_O1 + 4)
                wide_group(DN_O + 2 * t + 1, t, wo1)
                if t >= 1:
                    pe.wait_ge(xn_done, NT + t)
                    transpose_tile(O_ORDER["norm", t - 1], xn[0])
            pe.wait_ge(xn_done, 2 * NT)
            transpose_tile(O_ORDER["norm", 7], xn[0])

            def mlp_chunk(layer, c, tr_last, last=False):
                g0, u0 = UP_MLP[layer], U_MLP[layer]
                w1_units = (u0 + 8 * c - 1, u0 + 8 * c, u0 + 8 * c + 2, u0 + 8 * c + 4)
                for j in range(8):
                    f, half = divmod(j, 2)
                    need = [(w_lo, w1_units[f])] if half == 0 else []
                    if f == 0:
                        need.append((tr_lo, 2 * tr_last + (2 if half else 0)))
                    need.append((up_lo, g0 + 8 * c + j - 3))
                    up_group(g0 + j, w_slot[f % 2], half, need)
                for t in range(NT):
                    if t == 0:
                        pe.wait_ge(w_lo, u0 + 8 * c + (6 if last else 7))
                    if t % 4 == 0:
                        pe.wait_ge(up_lo, g0 + 8 * c + 7 + t // 4)
                    for half in range(2):
                        g = DN_MLP[layer] + 16 * c + 2 * t + half
                        pe.wait_ge(dn_used, g - 3)
                        pairs = [(tuple(a[:, f * T + t * P:f * T + (t + 1) * P] for a in (h1.hi, h1.lo)),
                                  tuple(a[:, half * HALF:(half + 1) * HALF] for a in (wide[f].hi, wide[f].lo))) for f in range(FT)]
                        three_passes(pe, bank(4 + (2 * t + half) % 4), pairs).then_inc(dn_full, 1)
                    if last and layer == 0 and t >= 1:
                        pe.wait_ge(xn_done, 2 * NT + t)
                        pool_tile(TR_POOL + t - 1, t - 1)

            for layer in range(2):
                tr_last = TR_POOL - 1 if layer == 0 else TR_MLP1 + NT - 1
                with pe.Fori(0, CHUNKS - 1) as c:
                    mlp_chunk(layer, c, tr_last)
                if layer == 0:
                    pe.wait_ge(band_in_s, 16)
                mlp_chunk(layer, CHUNKS - 1, tr_last, last=True)
                if layer == 0:
                    pe.wait_ge(xn_done, 3 * NT)
                    pool_tile(TR_POOL + 7, 7)
                    pe.wait_ge(w_lo, U_POOL + 2)
                    for t in range(NT):
                        pe.wait_ge(tr_lo, 2 * (TR_POOL + t) + 2)
                        for half in range(2):
                            g = DN_POOL + 2 * t + half
                            pe.wait_ge(dn_used, g - 3)
                            for grp in (2 * half, 2 * half + 1):
                                c0 = (grp % 2) * 2 * P
                                pairs = [(hT_parts(2 * grp + kt, t * P, P),
                                          tuple(a[:, grp * 2 * P:(grp + 1) * 2 * P] for a in (wide[kt].hi, wide[kt].lo))) for kt in range(2)]
                                mm = three_passes(pe, bank(4 + g % 4)[:, c0:c0 + 2 * P], pairs)
                            mm.then_inc(dn_full, 1)
                        if t >= 1:
                            pe.wait_ge(xn_done, 3 * NT + t)
                            transpose_tile(TR_MLP1 + t - 1, xn[0])
                    pe.wait_ge(xn_done, 4 * NT)
                    transpose_tile(TR_MLP1 + 7, xn[0])


_INS = ["x", "l0_norm_mix", "l0_fox_w_qkv", "l0_fox_w_f", "l0_fox_b_f", "l0_fox_w_o", "l0_norm_mlp", "l0_mlp_w1",
        "l0_mlp_w2", "l1_norm_mix", "l1_pool_w", "l1_pool_scale", "l1_norm_mlp", "l1_mlp_w1", "l1_mlp_w2", "final_norm"]


def kernel(**inputs):
    import concourse.bacc as _bacc
    from concourse.bass_utils import run_bass_kernel_spmd as _run

    nc = _bacc.Bacc("TRN2", target_bir_lowering=False, num_devices=1)
    arrays, args = {}, []
    values = {name: np.ascontiguousarray(inputs[name]) for name in _INS}
    values["const"], values["band"] = host_constants()
    for name, a in values.items():
        arrays[f"in_{name}"] = a
        args.append(nc.dram_tensor(f"in_{name}", a.shape, mybir.dt.from_np(a.dtype), kind="ExternalInput").ap())
    args.append(nc.dram_tensor("out", (1, T, D), F32, kind="ExternalOutput").ap())
    build(nc, *args)
    r = _run(nc, [arrays], core_ids=[0])
    return r.results[0]["out"]
```

```python
from contextlib import ExitStack

import numpy as np

import concourse.bass as bass
from concourse import mybir

F32 = mybir.dt.float32
F32R = mybir.dt.float32r
ACT = mybir.ActivationFunctionType
ALU = mybir.AluOpType

T = 1024
D = 1024
P = 128
NT = T // P
KD = D // P
HALF = 512
HEADS = 16
HD = 64
PAIRS = HEADS // 2
FF = 4096
CHUNK = 512
FT = CHUNK // P
CHUNKS = FF // CHUNK
SCALE = HD ** -0.5
EPS = 1e-6
NEG = -1e30
WINDOWS = (2, 4, 8, 16)
HALO = max(WINDOWS)
KB = 1024
ARENA = 206 * KB
HEAD_LOADS = 8
LATE_LOADS = 4
BAND = len(WINDOWS) * (2 * P + HALO)

U_V0, U_F, U_QK0, U_V1, U_QK, U_O0, U_O1 = 0, 4, 5, 7, 9, 25, 29
U_W1 = (33, 99)
U_POOL = 97
FILL = (12, 12, 6, 6, 6, 6, 6, 6, 6, 6, 6, 6, 6, 6, 0, 0)
GROUP = 3 * KD
K_SPLIT, Q_SPLIT = 2, 9
WO_STEPS = (2, 3, 7, 8, 9, 10, 11, 12, 13, 14)
FILL_END = {s: (sum(FILL[:s + 1]) // GROUP) - 1 for s in range(16) if FILL[s] and sum(FILL[:s + 1]) % GROUP == 0}
UP_QK, UP_MLP, UP_ALL = 0, (32, 96), 160
DN_V0, DN_V1, DN_O, DN_MLP, DN_POOL = 0, 8, 16, (32, 176), 160
TR_IN, TR_O, TR_POOL, TR_MLP1 = 0, 8, 24, 32


def o_phase_order():
    order = [("attn", 0)]
    for t in range(NT):
        if t + 1 < NT:
            order.append(("attn", t + 1))
        if t >= 1:
            order.append(("norm", t - 1))
    return order + [("norm", NT - 1)]


O_ORDER = {key: TR_O + n for n, key in enumerate(o_phase_order())}


def stage_count(u):
    return 16 * (u // 2 - 1)


def pool_bank(t, half):
    return (6 if t % 2 and t < NT - 1 else 4) + half


def up_bank(g):
    return g % 4


def wide_tile(p, s):
    q = s % 16
    return 8 * p + (8 * (s // 16) + 4 * (q // 8) + (q % 8 - 4))


def out_bank(s, last_pair):
    return 6 + s % 2 if last_pair and s >= 0 else 7


def host_constants():
    ident = np.eye(P, dtype=np.float32)
    row, col = np.arange(P)[:, None], np.arange(P)[None, :]
    mask = np.where(col > row, np.float32(NEG), np.float32(0))
    later, first, halo = [], [], []
    for w in WINDOWS:
        inside = (col - row >= 0) & (col - row < w)
        later.append(inside / w - ident)
        first.append(inside / np.minimum(col + 1, w) - ident)
        halo.append((np.arange(HALO)[None, :] + P - row < w) / w)
    band = np.concatenate([np.concatenate(m, 1) for m in (later, first, halo)], 1)
    return (np.concatenate([ident, mask], 1).astype(np.float32), band.astype(np.float32))


def build(nc, x, norm0, w_qkv, w_f, b_f, w_o, norm1, w1_0, w2_0, norm2, w_pool, pool_scale, norm3,
          w1_1, w2_1, norm4, const, band_in, out):
    gains = (norm0, norm1, norm2, norm3, norm4)
    w1s, w2s = (w1_0, w1_1), (w2_0, w2_1)
    ctx = ExitStack()
    with ctx:
        def sem(name):
            return ctx.enter_context(nc.semaphore(name))

        base = (nc.sbuf_base + 31) // 32 * 32
        ctx.enter_context(nc.sbuf_tensor("arena", [P, ARENA // 4], F32))

        def at(name, shape, dt, off):
            return nc.alloc_sbuf_tensor_at(name, shape, dt, offset=base + off)

        class Parts:
            def __init__(self, name, cols, off, lo_off=None):
                self.hi = at(name + "_hi", [P, cols], F32R, off)
                self.lo = at(name + "_lo", [P, cols], F32R, off + 4 * cols if lo_off is None else lo_off)

        A, B, C, DD, E, FF_, G = (n * KB for n in (0, 32, 96, 128, 144, 176, 184))
        x_sb = at("x_res", [P, NT * D], F32, A)
        v1_w = [Parts(f"wv1_{j}", 1024, A + 8 * KB * j) for j in range(4)]
        o_sb = at("attn_out", [P, NT * D], F32, A)
        hT = Parts("hT", KD * T, B)
        p_ring = [at(f"probs{i}", [P, T], F32, C + 4 * KB * i) for i in range(4)]
        pt_a = [at(f"probsT_a{i}", [P, HALF], F32, C + 16 * KB + 2 * KB * i) for i in range(2)]
        pt_b = [at(f"probsT_b{i}", [P, HALF], F32, C + 20 * KB + 2 * KB * i) for i in range(2)]
        qk_tmp = [Parts(f"qk_tmp{i}", HALF, C + 24 * KB + 4 * KB * i) for i in range(2)]
        v_tmp = [at(f"v_tmp{i}", [P, HALF], F32, C + 2 * KB * i) for i in range(4)]
        aT = Parts("aT", KD * T, C, E)
        h1 = Parts("hidden", FT * T, B)
        w2_t = [Parts(f"w2_{j}", 1024, B + 32 * KB + 8 * KB * j) for j in range(4)]
        wo_rest = [Parts(f"wo_{j}", 1024, B + 8 * KB * j) for j in range(6)]
        w_slot = [Parts(f"wslot{i}", 1024, DD + 8 * KB * i) for i in range(2)]
        mask_f32 = at("mask_f32", [P, P], F32, DD)
        y_ring = [at(f"y{i}", [P, D], F32, DD + 4 * KB * i) for i in range(2)]
        wide = [Parts(f"wide{j}", 1024, E + 8 * KB * j) for j in range(4)]
        qs = [at(f"q_stack{i}", [P, T], F32R, E + 16 * KB * i) for i in range(2)]
        kh2 = [at(f"k_hi2_{i}", [P, T], F32R, E + 16 * KB * i + 4 * KB) for i in range(2)]
        kl2 = [at(f"k_lo2_{i}", [P, T], F32R, E + 16 * KB * i + 8 * KB) for i in range(2)]
        decay = [at(f"decay{i}", [P, T], F32, E + 16 * KB * i + 12 * KB) for i in range(2)]
        stage = [at(f"stage{i}", [P, 1024], F32, FF_ + 4 * KB * i) for i in range(2)]
        xn = [at(f"xn{i}", [P, D], F32, G + 4 * KB * i) for i in range(2)]
        gain_sb = at("gain", [P, D], F32, G + 8 * KB)
        pscale_sb = at("pool_scale", [P, D], F32, G + 12 * KB)
        ident = at("ident", [P, P], F32, G + 16 * KB)
        ident_r = at("ident_r", [P, P], F32R, G + 16 * KB + 512)
        mask_r = at("mask_r", [P, P], F32R, G + 17 * KB)
        band = at("band", [P, BAND], F32, G + 17 * KB + 512)
        first_stage = [at(f"first_stage{i}", [P, 1024], F32, C + (8 + 4 * i) * KB) for i in range(4)]
        v_head = [at(f"v_head{i}", [P, NT * HD], F32, G + 17 * KB + 512 + 2 * KB * i) for i in range(2)]
        small = at("small", [P, 64], F32, G + 21 * KB + 768)
        ss, ms, rt, rs, nw = (small[:, i:i + 1] for i in (0, 1, 2, 3, 5))
        mark = small[:, 6:7]
        bf_sb = small[0:HEADS, 4:5]
        mx, negmx, rsum, rinv = (small[:, 8 + 8 * i:16 + 8 * i] for i in range(4))

        ps = ctx.enter_context(nc.psum_tensor("acc", [P, 8 * HALF], F32))

        def bank(b, n=1):
            return ps[:, b * HALF:(b + n) * HALF]

        q_parts = nc.dram_tensor("q_parts", [2, D, T], F32, kind="Internal").ap()
        k_parts = nc.dram_tensor("k_parts", [2, D, T], F32, kind="Internal").ap()
        v_dram = nc.dram_tensor("values", [T, D], F32, kind="Internal").ap()
        cum_dram = nc.dram_tensor("cum_decay", [HEADS, T], F32, kind="Internal").ap()

        const_in = sem("const_in")
        mask_in = sem("mask_in")
        bf_in = sem("bf_in")
        first_x_in, first_gain_in = sem("first_x_in"), sem("first_gain_in")
        gain_in = sem("gain_in")
        band_in_s = sem("band_loaded")
        pscale_in = sem("pscale_in")
        x_in = [sem(f"x_in{t}") for t in range(NT)]
        stage_in = [sem(f"stage_in{i}") for i in range(2)]
        first_stage_in = [sem(f"first_stage_in{i}") for i in range(4)]
        head_in = [sem(f"head_in{i}") for i in range(2)]
        head_late = [sem(f"head_late{i}") for i in range(2)]
        consts_ready = sem("consts_ready")
        stage_zeroed = sem("stage_zeroed")
        w_hi, w_lo = sem("w_hi"), sem("w_lo")
        sq_done, ms_done, rt_done, rs_done, xn_done = (sem(n) for n in ("sq_done", "ms_done", "rt_done", "rs_done", "xn_done"))
        tr_full, tr_hi, tr_lo = sem("tr_full"), sem("tr_hi"), sem("tr_lo")
        gate_full = sem("gate_full")
        up_full, up_act, up_hi, up_lo = sem("up_full"), sem("up_act"), sem("up_hi"), sem("up_lo")
        dn_full, dn_used = sem("dn_full"), sem("dn_used")
        pool_w_scaled = sem("pool_w_scaled")
        gate_act, gate_dve, gate_stored = sem("gate_act"), sem("gate_dve"), sem("gate_stored")
        qk_stored = [sem(f"qk_stored{i}") for i in range(2)]
        v_stored = [sem(f"v_stored{i}") for i in range(4)]
        s_full, bias_done, negmx_done, p_done = sem("s_full"), sem("bias_done"), sem("negmx_done"), sem("p_done")
        ta_full, tb_full, pta_done, ptb_done = sem("ta_full"), sem("tb_full"), sem("pta_done"), sem("ptb_done")
        wo_half_hi, wo_half_lo = sem("wo_half_hi"), sem("wo_half_lo")
        mark_done = sem("mark_done")
        o_full, rinv_done, o_done = sem("o_full"), sem("rinv_done"), sem("o_done")
        y_out = [sem(f"y_out{i}") for i in range(2)]

        block = ctx.enter_context(nc.Block())

        def unit_dst(u):
            if u < U_F:
                return wide[u - U_V0]
            if u == U_F:
                return w_slot[0]
            if u < U_V1:
                return w_slot[1 - (u - U_QK0)]
            if u < U_QK + 2:
                return v1_w[u - U_V1]
            if u < U_O0:
                return w_slot[1 - (u - U_QK) % 2]
            if u < U_W1[0]:
                return wo[u - U_O0]
            if u in (U_POOL, U_POOL + 1):
                return w_slot[u - U_POOL]
            return w1_first[u - (U_W1[1] if u >= U_W1[1] else U_W1[0])]

        wo = [w_slot[1], w_slot[0]] + wo_rest
        w1_first = [w2_t[2], w2_t[3], w_slot[0], w_slot[1]]

        def chunk_units(layer, c, kind):
            w2 = [("w2", f, 0, w2_t[f]) for f in range(FT)]
            ahead = [("w1", 0, 1, w_slot[0]), ("w1", 1, 1, w_slot[1])]
            now = [("w1", 2, 0, w_slot[0]), ("w1", 3, 0, w_slot[1])]
            if kind == "first":
                plan = [w2[0], w2[1], w2[2], w2[3], None, None] + ahead
            else:
                plan = [w2[0], w2[1]] + now + [w2[2], w2[3]] + (ahead if kind == "loop" else [None, None])
            n, out_plan = 0, []
            for item in plan:
                out_plan.append((n,) + item if item else None)
                n += bool(item)
            return U_W1[layer] + (4 if kind == "first" else 2), out_plan

        def mlp_bank(layer, kind, j):
            return 6 + j if layer == 1 and kind == "first" and j < 2 else up_bank(j)

        UP_ORDER = [(0, 0), (1, 0), (0, 1), (1, 1), (2, 0), (3, 0), (2, 1), (3, 1)]

        def three_passes(pe, dst, pairs, before=lambda k: None):
            n = 0
            for k, ((s_hi, s_lo), (m_hi, m_lo)) in enumerate(pairs):
                before(k)
                for s, m in ((s_lo, m_hi), (s_hi, m_lo), (s_hi, m_hi)):
                    mm = pe.matmul(dst, s, m, start=(n == 0), stop=(n == 3 * len(pairs) - 1))
                    n += 1
            return mm

        @block.sync
        def _(sp):
            def load_unit(u, parity, src, cols=None):
                if not isinstance(u, int) or u >= 6:
                    sp.wait_ge(w_lo, u - 1)
                dst = stage[parity][:, :] if cols is None else stage[parity][:, :].rearrange("p (k n) -> p k n", n=cols)
                sp.dma_start(dst, src).then_inc(stage_in[parity], 16)

            w_cols = lambda w, c0, n: w.rearrange("(k p) n -> p k n", p=P)[:, :, bass.ds(c0, n)]

            def load_wide(first, w, c0):
                for j in range(4):
                    load_unit(first + j, (first + j) % 2, w_cols(w, c0, HALF)[:, 2 * j:2 * j + 2, :], HALF)

            def store_parts(n_static, n, dram, p):
                slot, half = n_static % 2, n_static % 2
                sp.wait_ge(up_lo, n + 1)
                for part, t in enumerate((qk_tmp[slot].hi, qk_tmp[slot].lo)):
                    sp.dma_start(dram[part, bass.ds(p * P, P), half * HALF:(half + 1) * HALF],
                                 t[:, :].bitcast(F32)).then_inc(qk_stored[slot], 16)

            def store_group(p, j):
                store_parts(j, UP_QK + 4 * p + j, (q_parts, k_parts)[j // 2], p)

            def load_head(h, slot, k_ready=lambda: None):
                s = head_in[slot]

                def load_parts(half, dst, src, s, cols=slice(0, T)):
                    rows = slice(half * HD, (half + 1) * HD)
                    sp.dma_start(dst[slot][rows, cols].bitcast(F32), src[bass.ds(h * HD, HD), cols]).then_inc(s, 16)

                sp.dma_start(decay[slot][:, :], cum_dram[bass.ds(h, 1), :].to_broadcast([P, T])).then_inc(s, 16)
                sp.dma_start(v_head[slot][:, :].rearrange("p (k d) -> p k d", d=HD),
                             v_dram.rearrange("(k p) c -> p k c", p=P)[:, :, bass.ds(h * HD, HD)]).then_inc(s, 16)
                for half in range(2):
                    load_parts(half, qs, q_parts[half], s)
                for tokens, loaded in ((slice(0, HALF), s), (slice(HALF, T), head_late[slot])):
                    for half in range(2):
                        load_parts(half, kh2, k_parts[0], loaded, tokens)
                        load_parts(half, kl2, k_parts[1], loaded, tokens)
                    if loaded is s:
                        k_ready()

            sp.dma_start(x_sb[:, 0:D], x[0, 0:P, :]).then_inc(first_x_in, 16)
            sp.dma_start(gain_sb[:, :], gains[0].rearrange("(a n) -> a n", a=1).to_broadcast([P, D])).then_inc(first_gain_in, 16)
            for j in range(4):
                sp.dma_start(first_stage[j][:, :].rearrange("p (k n) -> p k n", n=HALF),
                             w_cols(w_qkv, 2 * D, HALF)[:, 2 * j:2 * j + 2, :]).then_inc(first_stage_in[j], 16)
            sp.wait_ge(stage_zeroed, 1)
            sp.wait_ge(w_lo, 2)
            sp.dma_start(stage[0][:, :].rearrange("p (k n) -> p k n", n=P)[:, :, 0:HEADS],
                         w_f.rearrange("(k p) n -> p k n", p=P)).then_inc(stage_in[0], 16)
            load_unit(U_QK0, U_QK0 % 2, w_cols(w_qkv, 0, P), P)
            load_unit(U_QK0 + 1, (U_QK0 + 1) % 2, w_cols(w_qkv, D, P), P)
            load_wide(U_V1, w_qkv, 2 * D + HALF)
            sp.wait_ge(gate_dve, 3)
            sp.dma_start(cum_dram[:, :], xn[0][0:HEADS, :]).then_inc(gate_stored, 16)
            load_unit(U_QK + 2, (U_QK + 2) % 2, w_cols(w_qkv, P, P), P)
            store_parts(0, UP_QK, q_parts, 0)
            store_parts(1, UP_QK + 1, q_parts, 0)
            load_unit(U_QK + 3, (U_QK + 3) % 2, w_cols(w_qkv, D + P, P), P)
            load_unit(U_QK + 4, (U_QK + 4) % 2, w_cols(w_qkv, 2 * P, P), P)
            store_parts(2, UP_QK + 2, k_parts, 0)
            store_parts(3, UP_QK + 3, k_parts, 0)

            def wait_stored(p, half):
                for s in qk_stored:
                    sp.wait_ge(s, 64 * p + (32 + 32 * half))

            wait_stored(0, 1)
            sp.wait_ge(gate_stored, 16)
            for s in v_stored:
                sp.wait_ge(s, 32)
            load_head(0, 0)
            load_head(1, 1)

            def wo_cols(j):
                return w_cols(w_o, 0, HALF)[:, 2 * j:2 * j + 2, :]

            def attention(p, first=False, k_src=None, q_src=None):
                u = U_QK + 5
                k_cols, q_cols = (w_cols(w_qkv, p * P + (D + 2 * P), P), P), (w_cols(w_qkv, p * P + 3 * P, P), P)
                load_unit(u + 2 * p, u % 2, *(k_src or k_cols))
                for j in range(3):
                    store_group(p + 1, j)
                if first:
                    for s in v_stored:
                        sp.wait_ge(s, 64)
                sp.wait_ge(o_full, 16 * p + 8)
                wait_stored(p + 1, 0)
                sp.wait_ge(qk_stored[0], 64 * p + 128)

                def k_ready():
                    store_group(p + 1, 3)
                    wait_stored(p + 1, 1)

                load_head(2 * p + 2, 0, k_ready)
                load_unit(u + 1 + 2 * p, (u + 1) % 2, *(q_src or q_cols))
                sp.wait_ge(o_full, 16 * p + 16)
                load_head(2 * p + 3, 1)

            attention(0, first=True)
            with sp.Fori(1, PAIRS - 3) as p:
                attention(p)
            attention(PAIRS - 3, q_src=(wo_cols(0), HALF))
            attention(PAIRS - 2, k_src=(wo_cols(1), HALF), q_src=(wo_cols(2), HALF))
            load_unit(U_O0 + 3, (U_O0 + 3) % 2, wo_cols(3), HALF)
            for j in range(4):
                load_unit(U_O1 + j, (U_O1 + j) % 2, w_cols(w_o, HALF, HALF)[:, 2 * j:2 * j + 2, :], HALF)

            def load_w1(u, parity, w, c, f):
                load_unit(u, parity, w_cols(w, c * CHUNK + f * P, P), P)

            def load_w2(u, parity, w, c, f):
                load_unit(u, parity, w[bass.ds(c * CHUNK + f * P, P), :])

            def mlp_units(layer, c, kind="loop"):
                u0, plan = chunk_units(layer, c, kind)
                for n, what, f, ahead, _ in filter(None, plan):
                    (load_w1 if what == "w1" else load_w2)(u0 + 8 * c + n, (u0 + n) % 2, (w1s if what == "w1" else w2s)[layer], c + ahead, f)

            for layer in range(2):
                if layer:
                    for j in range(2):
                        load_unit(U_POOL + j, (U_POOL + j) % 2,
                                  w_pool.rearrange("g (k p) o -> k p g o", p=P)[j], 2 * P)
                for f in range(FT):
                    load_w1(U_W1[layer] + f, (U_W1[layer] + f) % 2, w1s[layer], 0, f)
                mlp_units(layer, 0, "first")
                with sp.Fori(1, CHUNKS - 1) as c:
                    mlp_units(layer, c)
                mlp_units(layer, CHUNKS - 1, "last")
            for t in range(NT):
                sp.wait_ge(xn_done, 4 * NT + t + 1)
                sp.dma_start(out[0, t * P:(t + 1) * P, :], y_ring[t % 2][:, :]).then_inc(y_out[t % 2], 16)
            for s in y_out:
                sp.wait_ge(s, 16 * NT // 2)

        @block.gpsimd
        def _(gp):
            def load_gain(n):
                gp.dma_start(gain_sb[:, :], gains[n].rearrange("(a n) -> a n", a=1).to_broadcast([P, D])).then_inc(gain_in, 16)

            def load_x(t):
                gp.dma_start(x_sb[:, t * D:(t + 1) * D], x[0, t * P:(t + 1) * P, :]).then_inc(x_in[t], 16)

            def load_late_constants():
                gp.wait_ge(gate_dve, 3)
                load_gain(1)
                gp.dma_start(pscale_sb[:, :], pool_scale.rearrange("(a n) -> a n", a=1).to_broadcast([P, D])).then_inc(pscale_in, 16)

            gp.dma_start(ident[:, :], const[:, 0:P]).then_inc(const_in, 16)
            gp.memset(stage[0][:, :], 0.0).then_inc(stage_zeroed, 1)
            for t in range(1, NT):
                load_x(t)
            gp.dma_start(mask_f32[:, :], const[:, P:2 * P]).then_inc(mask_in, 16)
            gp.dma_start(bf_sb, b_f.rearrange("(a n) -> a n", n=1)).then_inc(bf_in, 16)
            for g in range(2 * NT):
                half, t = divmod(g, NT)
                if g == NT:
                    load_late_constants()
                gp.wait_ge(dn_used, g + 1)
                gp.dma_start(v_dram[t * P:(t + 1) * P, half * HALF:(half + 1) * HALF], v_tmp[g % 4][:, :]).then_inc(v_stored[g % 4], 16)
            for t in range(NT):
                gp.wait_ge(tr_full, O_ORDER["attn", t] + 1)
                load_x(t)
            gp.dma_start(band[:, :], band_in).then_inc(band_in_s, 16)
            for n in (2, 3, 4):
                gp.wait_ge(xn_done, NT * n)
                load_gain(n)

        @block.scalar
        def _(act):
            def split(u, parity, dst):
                act.wait_ge(stage_in[parity], stage_count(u) if isinstance(u, int) else u)
                act.activation(dst.hi[:, :], stage[parity][:, :], ACT.Copy).then_inc(w_hi, 1)

            def split_static(u):
                split(u, u % 2, unit_dst(u))

            def split_first(u):
                act.wait_ge(first_stage_in[u], 16)
                act.activation(unit_dst(u).hi[:, :], first_stage[u][:, :], ACT.Copy).then_inc(w_hi, 1)

            def norm_tile(n, t, ready=None, buf=None, buf_free=()):
                if ready is not None:
                    act.wait_ge(*ready)
                for w in buf_free:
                    act.wait_ge(*w)
                act.activation(buf[:, :], x_sb[:, t * D:(t + 1) * D], ACT.Square, accum_out=ss).then_inc(sq_done, 1)
                act.wait_ge(ms_done, n * NT + t + 1)
                act.activation(rt, ms, ACT.Sqrt).then_inc(rt_done, 1)

            def tr_evac(i, t, dst):
                act.wait_ge(tr_full, i + 1)
                for b in range(2):
                    act.activation(dst.hi[:, :].rearrange("p (k n) -> p k n", n=T)[:, 4 * b:4 * b + 4, t * P:(t + 1) * P],
                                   bank(2 * (i % 2) + b).rearrange("p (k n) -> p k n", n=P), ACT.Copy).then_inc(tr_hi, 1)

            def v_evac(g):
                act.wait_ge(dn_full, g + 1)
                if g >= 4:
                    act.wait_ge(v_stored[g % 4], 16 * (g // 4))
                act.activation(v_tmp[g % 4][:, :], bank(4 + g % 4), ACT.Copy).then_inc(dn_used, 1)

            def qk_evac(n_static, n, b, stored=None):
                if stored is not None:
                    act.wait_ge(qk_stored[n_static % 2], stored)
                act.wait_ge(up_full, n + 1)
                act.activation(qk_tmp[n_static % 2].hi[:, :], bank(b), ACT.Copy).then_inc(up_hi, 1)

            for t in range(NT):
                norm_tile(0, t, (x_in[t] if t else first_x_in, 16), xn[t % 2], [(tr_full, t - 1)] if t >= 2 else [])
                if t == 0:
                    split_first(0)
                    split_first(1)
                    tr_evac(TR_IN, 0, hT)
                    split_first(2)
                    split_first(3)
                if t >= 2:
                    tr_evac(TR_IN + t - 1, t - 1, hT)
                if t >= 2:
                    v_evac(t - 2)
            tr_evac(TR_IN + 7, 7, hT)
            act.wait_ge(mask_in, 16)
            act.wait_ge(const_in, 16)
            act.activation(mask_r[:, :], mask_f32[:, :], ACT.Copy).then_inc(consts_ready, 1)
            act.activation(ident_r[:, :], ident[:, :], ACT.Copy).then_inc(consts_ready, 1)
            act.wait_ge(consts_ready, 2)
            split_static(U_F)
            v_evac(6)
            v_evac(7)
            split_static(U_QK0)
            gate_ps = bank(2, 2)[0:HEADS, :]
            act.wait_ge(bf_in, 16)
            act.wait_ge(gate_full, 2)
            act.activation(xn[0][0:HEADS, :], gate_ps, ACT.Abs, bias=bf_sb).then_inc(gate_act, 1)
            act.wait_ge(gate_act, 1)
            act.activation(xn[0][0:HEADS, :], xn[0][0:HEADS, :], ACT.Exp, scale=-1.0).then_inc(gate_act, 1)
            act.wait_ge(gate_act, 2)
            act.activation(xn[0][0:HEADS, :], xn[0][0:HEADS, :], ACT.Ln, bias=1.0).then_inc(gate_act, 1)
            split_static(U_QK0 + 1)
            act.wait_ge(xn_done, NT)
            split_static(U_V1)
            qk_evac(0, UP_QK, up_bank(0))
            split_static(U_V1 + 1)
            qk_evac(1, UP_QK + 1, up_bank(1))
            split_static(U_V1 + 2)
            split_static(U_V1 + 3)
            split_static(U_QK + 2)
            qk_evac(2, UP_QK + 2, up_bank(2), 32)
            qk_evac(3, UP_QK + 3, up_bank(3), 32)
            for t in range(NT):
                v_evac(DN_V1 + t)

            def exp_tile(p, s, first):
                j, w = 16 * p + s, (s % 8 + 1) * P
                act.wait_ge(negmx_done, j + 1)
                if not first or s >= 4:
                    if (s - 4) % 8 < 4:
                        act.wait_ge(ta_full, j - 3)
                    else:
                        act.wait_ge(tb_full, wide_tile(p, s - 4) + 1)
                if not first or s >= 8:
                    act.wait_ge(o_done, j - 7)
                act.activation(p_ring[s % 4][:, 0:w], bank(2 * (s % 2), 2)[:, 0:w], ACT.Exp,
                               bias=negmx[:, s % 8:s % 8 + 1], scale=SCALE,
                               accum_out=rsum[:, s % 8:s % 8 + 1]).then_inc(p_done, 1)

            def evac_a(p, s, first=False):
                j, w = 16 * p + s, min(s % 8 + 1, 4) * P
                act.wait_ge(ta_full, j + 1)
                if not first or s >= 2:
                    act.wait_ge(o_full, j - 1)
                act.activation(pt_a[s % 2][:, 0:w], bank(4)[:, 0:w], ACT.Copy).then_inc(pta_done, 1)

            def attention(p, first=False, last=False):
                for s in range(16):
                    if not first or s >= 2:
                        evac_a(p, s - 2, first)
                    exp_tile(p, s, first)
                    if not last and s in FILL_END:
                        j = FILL_END[s]
                        qk_evac(j, UP_QK + 4 * p + (j + 4), 6, 64 * p + (64 + 32 * (j // 2)))
                    if s == K_SPLIT or (s == Q_SPLIT and not last):
                        u = U_QK + 3 + (s == Q_SPLIT)
                        act.wait_ge(stage_in[u % 2], 16 * p + stage_count(u))
                        act.activation(w_slot[u % 2].hi[:, :], stage[u % 2][:, :], ACT.Copy).then_inc(w_hi, 1)
                    if last and s in WO_STEPS:
                        n, half = divmod(WO_STEPS.index(s), 2)
                        u, cols = U_O0 + 2 + n, slice(half * HALF, (half + 1) * HALF)
                        act.wait_ge(stage_in[u % 2], stage_count(u))
                        act.activation(unit_dst(u).hi[:, cols], stage[u % 2][:, cols], ACT.Copy).then_inc(w_hi if half else wo_half_hi, 1)

            for s in v_stored:
                act.wait_ge(s, 64)
            attention(0, first=True)
            with act.Fori(1, PAIRS - 1) as p:
                attention(p)
            attention(PAIRS - 1, last=True)
            for s in (14, 15):
                evac_a(PAIRS - 1, s)
            split_static(U_W1[0] - 1)

            act.wait_ge(o_full, 8 * HEADS)
            tr_evac(O_ORDER["attn", 0], 0, aT)
            for t in range(NT):
                if t + 1 < NT:
                    tr_evac(O_ORDER["attn", t + 1], t + 1, aT)
                else:
                    tr_evac(O_ORDER["norm", t - 1], t - 1, aT)
                if t == NT - 2:
                    split_static(U_W1[0])
                    split_static(U_W1[0] + 1)
                norm_tile(1, t, (dn_used, DN_O + 2 * t + 2), xn[t % 2],
                          [(tr_full, O_ORDER["norm", t - 2] + 1)] if t >= 2 else [(gate_stored, 16)])
                if 1 <= t < NT - 1:
                    tr_evac(O_ORDER["norm", t - 1], t - 1, aT)
            tr_evac(O_ORDER["norm", 7], 7, aT)
            act.wait_ge(dn_full, DN_O + 16)
            split_static(U_W1[0] + 2)
            split_static(U_W1[0] + 3)

            def mlp_up(layer, c, kind="loop"):
                g0 = UP_MLP[layer]
                u0, plan = chunk_units(layer, c, kind)
                for j, (f, half) in enumerate(UP_ORDER):
                    b = bank(mlp_bank(layer, kind, j))
                    g = g0 + 8 * c + j
                    act.wait_ge(up_full, g + 1)
                    act.activation(b, b, ACT.Relu).then_inc(up_act, 1)
                    act.wait_ge(up_act, 2 * (g - UP_MLP[0]) + 1)
                    act.activation(b, b, ACT.Square).then_inc(up_act, 1)
                    act.wait_ge(up_act, 2 * (g - UP_MLP[0]) + 2)
                    act.activation(h1.hi[:, f * T + half * HALF:f * T + (half + 1) * HALF], b, ACT.Copy).then_inc(up_hi, 1)
                    if plan[j]:
                        n, _, _, _, dst = plan[j]
                        act.wait_ge(stage_in[(u0 + n) % 2], 64 * c + stage_count(u0 + n))
                        act.activation(dst.hi[:, :], stage[(u0 + n) % 2][:, :], ACT.Copy).then_inc(w_hi, 1)

            for layer in range(2):
                mlp_up(layer, 0, "first")
                with act.Fori(1, CHUNKS - 1) as c:
                    mlp_up(layer, c)
                mlp_up(layer, CHUNKS - 1, "last")
                dn0 = DN_MLP[layer] + 16 * (CHUNKS - 1)
                if layer == 0:
                    for t in range(NT):
                        if t in (2, 3):
                            act.wait_ge(pool_w_scaled, t - 1)
                            act.activation(unit_dst(U_POOL + t - 2).hi[:, :], stage[(U_POOL + t - 2) % 2][:, :], ACT.Copy).then_inc(w_hi, 1)
                        norm_tile(2, t, (dn_used, dn0 + 2 * t + 2), xn[t % 2], [(tr_full, TR_POOL + t)])
                        if t >= 1:
                            tr_evac(TR_POOL + t - 1, t - 1, aT)
                    tr_evac(TR_POOL + 7, 7, aT)
                    for t in range(NT):
                        norm_tile(3, t, (dn_used, DN_POOL + 2 * t + 2), xn[t % 2],
                                  [(tr_full, TR_MLP1 + max(t - 1, 0))])
                        if t >= 1:
                            tr_evac(TR_MLP1 + t - 1, t - 1, aT)
                        if t in (2, 4):
                            split_static(U_W1[1] + t // 2 - 1)
                    tr_evac(TR_MLP1 + 7, 7, aT)
                    act.wait_ge(dn_full, DN_POOL + 16)
                    split_static(U_W1[1] + 2)
                    split_static(U_W1[1] + 3)
                else:
                    for t in range(NT):
                        norm_tile(4, t, (dn_used, dn0 + 2 * t + 2), y_ring[t % 2],
                                  [(y_out[t % 2], 16 * (t // 2))] if t >= 2 else [])

        @block.vector
        def _(dve):
            def split(u_next, parity, dst):
                dve.wait_ge(w_hi, u_next)
                dve.tensor_tensor(dst.lo[:, :], stage[parity][:, :], dst.hi[:, :].bitcast(F32), ALU.subtract).then_inc(w_lo, 1)

            def split_static(u):
                split(u + 1, u % 2, unit_dst(u))

            def split_first(u):
                dve.wait_ge(w_hi, u + 1)
                dve.tensor_tensor(unit_dst(u).lo[:, :], first_stage[u][:, :], unit_dst(u).hi[:, :].bitcast(F32), ALU.subtract).then_inc(w_lo, 1)

            def norm_tile(n, t, dst):
                i = n * NT + t + 1
                dve.wait_ge(sq_done, i)
                dve.tensor_scalar(ms, ss, 1.0 / D, EPS, ALU.mult, ALU.add).then_inc(ms_done, 1)
                dve.wait_ge(rt_done, i)
                if i > 1:
                    dve.wait_ge(xn_done, i - 1)
                dve.reciprocal(rs, rt).then_inc(rs_done, 1)
                dve.wait_ge(rs_done, 4 * i - 3)
                dve.tensor_scalar(nw, ms, rs, rs, ALU.mult, ALU.mult).then_inc(rs_done, 1)
                dve.wait_ge(rs_done, 4 * i - 2)
                dve.tensor_scalar(nw, nw, -0.5, 1.5, ALU.mult, ALU.add).then_inc(rs_done, 1)
                dve.wait_ge(rs_done, 4 * i - 1)
                dve.tensor_scalar(rs, nw, rs, None, ALU.mult).then_inc(rs_done, 1)
                dve.wait_ge(rs_done, 4 * i)
                if t == 0:
                    dve.wait_ge(*((gain_in, 16 * n) if n else (first_gain_in, 16)))
                dve.scalar_tensor_tensor(dst[:, :], x_sb[:, t * D:(t + 1) * D], rs, gain_sb[:, :],
                                         ALU.mult, ALU.mult).then_inc(xn_done, 1)

            def tr_evac(i, t, dst):
                for b in range(2):
                    dve.wait_ge(tr_hi, 2 * i + b + 1)
                    cols = lambda a: a[:, :].rearrange("p (k n) -> p k n", n=T)[:, 4 * b:4 * b + 4, t * P:(t + 1) * P]
                    dve.tensor_tensor(cols(dst.lo), bank(2 * (i % 2) + b).rearrange("p (k n) -> p k n", n=P),
                                      cols(dst.hi).bitcast(F32), ALU.subtract).then_inc(tr_lo, 1)

            def up_evac(g, b, hi, lo):
                dve.wait_ge(up_hi, g + 1)
                dve.tensor_tensor(lo, bank(b), hi.bitcast(F32), ALU.subtract).then_inc(up_lo, 1)

            def add_group(g, j, b=None):
                t, half = divmod(j, 2)
                b = 4 + j % 4 if b is None else b
                xs = x_sb[:, t * D + half * HALF:t * D + (half + 1) * HALF]
                dve.wait_ge(dn_full, g + 1)
                dve.wait_ge(dn_used, g - 15)
                dve.tensor_tensor(xs, bank(b), xs, ALU.add).then_inc(dn_used, 1)

            for t in range(NT):
                norm_tile(0, t, xn[t % 2])
                if t == 0:
                    split_first(0)
                    split_first(1)
                    tr_evac(TR_IN, 0, hT)
                    split_first(2)
                    split_first(3)
                if t >= 2:
                    tr_evac(TR_IN + t - 1, t - 1, hT)
            tr_evac(TR_IN + 7, 7, hT)
            split_static(U_F)
            split_static(U_QK0)
            gate_ps = bank(2, 2)[0:HEADS, :]
            dve.wait_ge(gate_act, 1)
            dve.tensor_scalar(gain_sb[0:HEADS, :], gate_ps, bf_sb, 0.0, ALU.add, ALU.min).then_inc(gate_dve, 1)
            dve.wait_ge(gate_act, 3)
            dve.wait_ge(gate_dve, 1)
            dve.tensor_tensor_scan(gate_ps, gain_sb[0:HEADS, :], xn[0][0:HEADS, :], 0.0, ALU.add, ALU.subtract).then_inc(gate_dve, 1)
            dve.wait_ge(gate_dve, 2)
            dve.tensor_scalar(xn[0][0:HEADS, :], gate_ps, -1.0 / SCALE, None, ALU.mult).then_inc(gate_dve, 1)
            split_static(U_QK0 + 1)

            def qk_evac(n_static, n, b):
                tmp = qk_tmp[n_static % 2]
                dve.wait_ge(up_hi, n + 1)
                dve.tensor_tensor(tmp.lo[:, :], bank(b), tmp.hi[:, :].bitcast(F32), ALU.subtract).then_inc(up_lo, 1)

            split_static(U_V1)
            qk_evac(0, UP_QK, up_bank(0))
            split_static(U_V1 + 1)
            qk_evac(1, UP_QK + 1, up_bank(1))
            split_static(U_V1 + 2)
            split_static(U_V1 + 3)
            split_static(U_QK + 2)
            qk_evac(2, UP_QK + 2, up_bank(2))
            qk_evac(3, UP_QK + 3, up_bank(3))

            def row_sum_inverse(p, s):
                j, q = 16 * p + s, s % 16
                dve.wait_ge(o_full, j + 1)
                dve.reciprocal(rinv[:, q % 8:q % 8 + 1], rsum[:, q % 8:q % 8 + 1]).then_inc(rinv_done, 1)

            def bias_tile(p, s, first):
                j, w = 16 * p + s, (s % 8 + 1) * P
                sc = bank(2 * (s % 2), 2)[:, 0:w]
                if s % 8 == 0:
                    dve.wait_ge(head_in[s // 8], 16 * HEAD_LOADS * p + 16 * HEAD_LOADS)
                dve.wait_ge(s_full, j + 1)
                dve.memset(mark, 0.0).then_inc(mark_done, 1)
                dve.tensor_tensor_reduce(out=sc, in0=sc, in1=decay[s // 8][:, 0:w], scale=1.0, scalar=-3.0e38,
                                         op0=ALU.add, op1=ALU.max, accum_out=mx[:, s % 8:s % 8 + 1]).then_inc(bias_done, 1)
                dve.wait_ge(bias_done, j + 1)
                dve.tensor_scalar(negmx[:, s % 8:s % 8 + 1], mx[:, s % 8:s % 8 + 1], -SCALE, None, ALU.mult).then_inc(negmx_done, 1)

            def evac_b(p, s, first=False):
                j, w = 16 * p + s, (s % 8 + 1 - 4) * P
                dve.wait_ge(tb_full, wide_tile(p, s) + 1)
                if not (first and s < 6):
                    dve.wait_ge(o_full, j - 5 if s % 8 < 6 else j - 1)
                dve.tensor_copy(pt_b[s % 2][:, 0:w], bank(5)[:, 0:w]).then_inc(ptb_done, 1)

            def out_tile(p, s, last=False):
                j, q = 16 * p + s, s % 16
                dve.wait_ge(rinv_done, j + 1)
                dve.tensor_scalar(o_sb[:, bass.ds(p * P + (s // 16 * P + (q % 8) * D + (q // 8) * HD), HD)],
                                  bank(out_bank(s, last))[:, 0:HD], rinv[:, q % 8:q % 8 + 1], None, ALU.mult).then_inc(o_done, 1)

            def attention(p, first=False, last=False):
                for s in range(16):
                    if not first or s >= 4:
                        row_sum_inverse(p, s - 4)
                        out_tile(p, s - 4, last)
                    bias_tile(p, s, first)
                    if (s - 2) % 8 >= 4 and (not first or s >= 2):
                        evac_b(p, s - 2, first)
                    ended = FILL_END.get(s) if FILL_END.get(s) != 3 else None
                    if FILL_END.get(s - 1) == 3:
                        ended = 3
                    if not last and ended is not None:
                        qk_evac(ended, UP_QK + 4 * p + (ended + 4), 6)
                    if s == K_SPLIT + 1 or (s == Q_SPLIT + 1 and not last):
                        u = U_QK + 3 + (s == Q_SPLIT + 1)
                        split(u + 1 + 2 * p, u % 2, w_slot[u % 2])
                    if last and s - 1 in WO_STEPS:
                        wo_half(WO_STEPS.index(s - 1))

            def wo_half(i):
                n, half = divmod(i, 2)
                u, cols = U_O0 + 2 + n, slice(half * HALF, (half + 1) * HALF)
                dst = unit_dst(u)
                dve.wait_ge(*((w_hi, u + 1) if half else (wo_half_hi, n + 1)))
                dve.tensor_tensor(dst.lo[:, cols], stage[u % 2][:, cols], dst.hi[:, cols].bitcast(F32),
                                  ALU.subtract).then_inc(w_lo if half else wo_half_lo, 1)

            attention(0, first=True)
            with dve.Fori(1, PAIRS - 1) as p:
                attention(p)
            attention(PAIRS - 1, last=True)
            last = PAIRS - 1
            evac_b(last, 14)
            row_sum_inverse(last, 12)
            out_tile(last, 12, True)
            evac_b(last, 15)
            for s in (13, 14, 15):
                row_sum_inverse(last, s)
                out_tile(last, s, True)
            split_static(U_W1[0] - 1)

            tr_evac(O_ORDER["attn", 0], 0, aT)
            for t in range(NT):
                if t + 1 < NT:
                    tr_evac(O_ORDER["attn", t + 1], t + 1, aT)
                dve.wait_ge(x_in[t], 32 if t else 16)
                add_group(DN_O + 2 * t, 2 * t)
                if t == NT - 1:
                    tr_evac(O_ORDER["norm", t - 1], t - 1, aT)
                add_group(DN_O + 2 * t + 1, 2 * t + 1)
                if t == NT - 2:
                    split_static(U_W1[0])
                    split_static(U_W1[0] + 1)
                norm_tile(1, t, xn[t % 2])
                if 1 <= t < NT - 1:
                    tr_evac(O_ORDER["norm", t - 1], t - 1, aT)
            tr_evac(O_ORDER["norm", 7], 7, aT)
            split_static(U_W1[0] + 2)
            split_static(U_W1[0] + 3)

            def mlp_up(layer, c, kind="loop"):
                g0 = UP_MLP[layer]
                u0, plan = chunk_units(layer, c, kind)
                for j, (f, half) in enumerate(UP_ORDER):
                    cols = slice(f * T + half * HALF, f * T + (half + 1) * HALF)
                    up_evac(g0 + 8 * c + j, mlp_bank(layer, kind, j), h1.hi[:, cols], h1.lo[:, cols])
                    if plan[j]:
                        n, _, _, _, dst = plan[j]
                        split(u0 + n + 1 + 8 * c, (u0 + n) % 2, dst)

            for layer in range(2):
                mlp_up(layer, 0, "first")
                for j in range(16):
                    add_group(DN_MLP[layer] + j, j)
                with dve.Fori(1, CHUNKS - 1) as c:
                    mlp_up(layer, c)
                    for j in range(16):
                        add_group(DN_MLP[layer] + 16 * c + j, j)
                mlp_up(layer, CHUNKS - 1, "last")
                dn0 = DN_MLP[layer] + 16 * (CHUNKS - 1)
                for t in range(NT):
                    for j in (2 * t, 2 * t + 1):
                        add_group(dn0 + j, j)
                    if layer == 0 and t in (1, 2):
                        u = U_POOL + t - 1
                        dve.wait_ge(pscale_in, 16)
                        dve.wait_ge(stage_in[u % 2], stage_count(u))
                        dve.tensor_tensor(stage[u % 2][:, :], stage[u % 2][:, :], pscale_sb[:, :], ALU.mult).then_inc(pool_w_scaled, 1)
                    if layer == 0 and t in (3, 4):
                        split_static(U_POOL + t - 3)
                    if layer == 0:
                        norm_tile(2, t, xn[t % 2])
                        if t >= 1:
                            tr_evac(TR_POOL + t - 1, t - 1, aT)
                    else:
                        norm_tile(4, t, y_ring[t % 2])
                if layer == 0:
                    pool_adds = lambda t: [add_group(DN_POOL + 2 * t + half, 2 * t + half, pool_bank(t, half)) for half in range(2)]
                    pool_adds(0)
                    tr_evac(TR_POOL + 7, 7, aT)
                    for t in range(NT):
                        if t + 1 < NT:
                            pool_adds(t + 1)
                        norm_tile(3, t, xn[t % 2])
                        if t >= 1:
                            tr_evac(TR_MLP1 + t - 1, t - 1, aT)
                        if t in (2, 4):
                            split_static(U_W1[1] + t // 2 - 1)
                    tr_evac(TR_MLP1 + 7, 7, aT)
                    split_static(U_W1[1] + 2)
                    split_static(U_W1[1] + 3)

        @block.tensor
        def _(pe):
            parts = lambda src, k, c0, n: tuple(a[:, k * T + c0:k * T + c0 + n] for a in (src.hi, src.lo))

            def tr_start(i, banks_free=()):
                for w in banks_free:
                    pe.wait_ge(*w)
                if i >= 2:
                    pe.wait_ge(tr_lo, 2 * (i - 2) + 2)

            def transpose_tile(i, src, banks_free=()):
                tr_start(i, banks_free)
                for k in range(KD):
                    dst = bank(2 * (i % 2) + k // 4)[:, (k % 4) * P:(k % 4 + 1) * P]
                    mm = pe.transpose(dst, src[:, k * P:(k + 1) * P], ident[:, :])
                mm.then_inc(tr_full, 1)

            def pool_tile(i, t):
                tr_start(i, [(up_lo, UP_MLP[1])] if t < 2 else [])
                for k in range(KD):
                    g = k // 2
                    dst = bank(2 * (i % 2) + k // 4)[:, (k % 4) * P:(k % 4 + 1) * P]
                    m0 = (g if t else len(WINDOWS) + g) * P
                    mm = pe.matmul(dst, xn[t % 2][:, k * P:(k + 1) * P], band[:, m0:m0 + P], start=True, stop=(t == 0))
                    if t:
                        h0 = 2 * len(WINDOWS) * P + g * HALO
                        mm = pe.matmul(dst[:, 0:HALO], xn[(t - 1) % 2][:, k * P:(k + 1) * P], band[:, h0:h0 + HALO],
                                       start=False, stop=True)
                mm.then_inc(tr_full, 1)

            def wide_group(g, t, tiles, src=None, units_from=None):
                if g >= 4:
                    pe.wait_ge(dn_used, g - 3)
                pairs = [(parts(src or hT, k, t * P, P), tuple(a[:, (k % 2) * HALF:(k % 2 + 1) * HALF]
                                                      for a in (tiles[k // 2].hi, tiles[k // 2].lo))) for k in range(KD)]
                before = lambda k: pe.wait_ge(w_lo, units_from + k // 2 + 1) if units_from is not None and k % 2 == 0 else None
                three_passes(pe, bank(4 + g % 4), pairs, before).then_inc(dn_full, 1)

            def up_group(b, slot, half, need, full=up_full, src=None):
                for w in need:
                    pe.wait_ge(*w)
                pairs = [(tuple(a[:, k * P:(k + 1) * P] for a in (slot.hi, slot.lo)), parts(src or hT, k, half * HALF, HALF)) for k in range(KD)]
                three_passes(pe, bank(b), pairs).then_inc(full, 1)

            pe.wait_ge(const_in, 16)
            for t in range(NT):
                if t != 1:
                    pe.wait_ge(xn_done, t + 1)
                    transpose_tile(TR_IN + t, xn[t % 2])
                if t >= 1:
                    pe.wait_ge(tr_lo, 2 * t)
                    wide_group(DN_V0 + t - 1, t - 1, wide, units_from=U_V0 if t == 1 else None)
                if t == 1:
                    pe.wait_ge(xn_done, t + 1)
                    transpose_tile(TR_IN + t, xn[t % 2])
            pe.wait_ge(tr_lo, 2 * NT)
            wide_group(DN_V0 + 7, 7, wide)
            for half in range(2):
                up_group(2 + half, w_slot[0], half, [(w_lo, U_F + 1)], gate_full)
            for j in range(4):
                up_group(up_bank(UP_QK + j), w_slot[1 - j // 2], j % 2,
                         [(w_lo, U_QK0 + j // 2 + 1)] + ([(gate_dve, 3)] if j == 2 else []))
            pe.wait_ge(w_lo, U_V1 + 4)
            for t in range(NT):
                wide_group(DN_V1 + t, t, v1_w)

            def next_pair_products(p, s):
                done = sum(FILL[:s])
                for n in range(done, done + FILL[s]):
                    j, i = divmod(n, GROUP)
                    k, part = divmod(i, 3)
                    if i == 0:
                        pe.wait_ge(w_lo, 2 * p + (U_QK + 3 + j // 2))
                        pe.wait_ge(up_lo, UP_QK + 4 * p + (j + 4))
                    w, a = w_slot[1 - j // 2], (hT.hi, hT.lo)
                    mm = pe.matmul(bank(6), ((w.lo, w.hi, w.hi)[part])[:, k * P:(k + 1) * P],
                                   a[part == 1][:, k * T + j % 2 * HALF:k * T + (j % 2 + 1) * HALF],
                                   start=(i == 0), stop=(i == GROUP - 1))
                if FILL[s] and s in FILL_END:
                    mm.then_inc(up_full, 1)

            def scores(j, s, first, head_count, late_count):
                i, slot = s % 8, s // 8
                w = (i + 1) * P
                if i == 0:
                    pe.wait_ge(head_in[slot], head_count)
                if i == HALF // P:
                    pe.wait_ge(head_late[slot], late_count)
                if not first or s >= 2:
                    pe.wait_ge(p_done, j - 1)
                q = qs[slot][:, i * P:(i + 1) * P]
                for c0 in range(0, w, HALF):
                    n = min(HALF, w - c0)
                    dst = bank(2 * (s % 2), 2)[:, c0:c0 + n]
                    diag = c0 + n == w
                    pe.matmul(dst, q, kl2[slot][:, c0:c0 + n], start=True, stop=False)
                    mm = pe.matmul(dst, q, kh2[slot][:, c0:c0 + n], start=False, stop=not diag)
                    if diag:
                        mm = pe.matmul(dst[:, n - P:n], ident_r[:, :], mask_r[:, :], start=False, stop=True)
                mm.then_inc(s_full, 1)

            def transposes(p, s, first=False):
                j, q = 16 * p + s, s % 16
                i = q % 8
                pe.wait_ge(p_done, j + 1)
                if not first or s >= 1:
                    pe.wait_ge(pta_done, j)
                for kt in range(min(i + 1, 4)):
                    mm = pe.transpose(bank(4)[:, kt * P:(kt + 1) * P], p_ring[q % 4][:, kt * P:(kt + 1) * P], ident[:, :])
                mm.then_inc(ta_full, 1)
                if i >= 4:
                    if not (first and s == 4):
                        pe.wait_ge(ptb_done, wide_tile(p, s))
                    for kt in range(4, i + 1):
                        mm = pe.transpose(bank(5)[:, (kt - 4) * P:(kt - 3) * P], p_ring[q % 4][:, kt * P:(kt + 1) * P], ident[:, :])
                    mm.then_inc(tb_full, 1)

            def weighted_values(p, s, first=False, last=False):
                j, q = 16 * p + s, s % 16
                i, slot = q % 8, q // 8
                pe.wait_ge(pta_done, j + 1)
                if i >= 4:
                    pe.wait_ge(ptb_done, wide_tile(p, s) + 1)
                if last and s >= 0:
                    pe.wait_ge(o_done, j - 1)
                elif not first or s >= 1:
                    pe.wait_ge(o_done, j)
                for kt in range(i + 1):
                    src = (pt_a if kt < 4 else pt_b)[q % 2][:, (kt % 4) * P:(kt % 4 + 1) * P]
                    mm = pe.matmul(bank(out_bank(s, last))[:, 0:HD], src, v_head[slot][:, kt * HD:(kt + 1) * HD],
                                   start=(kt == 0), stop=(kt == i))
                mm.then_inc(o_full, 1)

            def attention(p, first=False, last=False):
                for s in range(16):
                    scores(16 * p + s, s, first, 16 * HEAD_LOADS * p + 16 * HEAD_LOADS, 16 * LATE_LOADS * p + 16 * LATE_LOADS)
                    if first and s == 0:
                        pe.wait_ge(dn_used, DN_O)
                    if not first or s >= 2:
                        transposes(p, s - 2, first)
                    if not last:
                        next_pair_products(p, s)
                    if not first or s >= 3:
                        weighted_values(p, s - 3, first, last)

            pe.wait_ge(consts_ready, 2)
            pe.wait_ge(up_lo, UP_QK + 4)
            attention(0, first=True)
            with pe.Fori(1, PAIRS - 1) as p:
                attention(p)
            pe.wait_ge(up_lo, UP_MLP[0])
            attention(PAIRS - 1, last=True)
            last = PAIRS - 1
            transposes(last, 14)
            weighted_values(last, 13, last=True)
            transposes(last, 15)
            weighted_values(last, 14, last=True)
            weighted_values(last, 15, last=True)

            def attn_tile(t):
                transpose_tile(O_ORDER["attn", t], o_sb[:, t * D:(t + 1) * D], [(o_done, 8 * HEADS)])

            attn_tile(0)
            for t in range(NT):
                if t + 1 < NT:
                    attn_tile(t + 1)
                pe.wait_ge(tr_lo, 2 * O_ORDER["attn", t] + 2)
                pe.wait_ge(w_lo, U_O0 + 4)
                wide_group(DN_O + 2 * t, t, wo[:4], aT)
                if t == NT - 1:
                    pe.wait_ge(xn_done, NT + t)
                    transpose_tile(O_ORDER["norm", t - 1], xn[(t - 1) % 2])
                pe.wait_ge(w_lo, U_O1 + 4)
                wide_group(DN_O + 2 * t + 1, t, wo[4:], aT)
                if 1 <= t < NT - 1:
                    pe.wait_ge(xn_done, NT + t)
                    transpose_tile(O_ORDER["norm", t - 1], xn[(t - 1) % 2])

            def mlp_chunk(layer, c, kind="loop"):
                g0 = UP_MLP[layer]
                u0, _ = chunk_units(layer, c, kind)
                last = kind == "last"
                w1_units = (tuple(U_W1[layer] + f + 1 for f in range(FT)) if kind == "first" else
                            tuple(u0 + 8 * c + n for n in (-1, 0, 3, 4)))
                w1_tiles = w1_first if kind == "first" else [w_slot[f % 2] for f in range(FT)]
                tr_last = (O_ORDER["norm", NT - 1], TR_MLP1 + NT - 1)[layer]
                for j, (f, half) in enumerate(UP_ORDER):
                    if kind == "first" and layer == 1 and j < 2:
                        continue
                    need = [(w_lo, w1_units[f])] if half == 0 else []
                    if kind == "first" and j in (0, 2):
                        need.append((tr_lo, 2 * tr_last + (2 if half else 0)))
                    need.append((up_lo, g0 + 8 * c + j - 3))
                    up_group(mlp_bank(layer, kind, j), w1_tiles[f], half, need, src=aT)
                    if kind == "first" and j == 0:
                        pe.wait_ge(xn_done, 2 * NT)
                        transpose_tile(tr_last, xn[(NT - 1) % 2])
                for t in range(NT):
                    if t == 0:
                        pe.wait_ge(w_lo, u0 + 8 * c + (4 if kind == "first" else 6))
                    if t % 4 == 0:
                        pe.wait_ge(up_lo, g0 + 8 * c + 6 + t // 2)
                    for half in range(2):
                        g = DN_MLP[layer] + 16 * c + 2 * t + half
                        pe.wait_ge(dn_used, g - 3)
                        pairs = [(tuple(a[:, f * T + t * P:f * T + (t + 1) * P] for a in (h1.hi, h1.lo)),
                                  tuple(a[:, half * HALF:(half + 1) * HALF] for a in (w2_t[f].hi, w2_t[f].lo))) for f in range(FT)]
                        three_passes(pe, bank(4 + (2 * t + half) % 4), pairs).then_inc(dn_full, 1)
                    if last and layer == 0 and t >= 1:
                        pe.wait_ge(xn_done, 2 * NT + t)
                        pool_tile(TR_POOL + t - 1, t - 1)

            for layer in range(2):
                mlp_chunk(layer, 0, "first")
                with pe.Fori(1, CHUNKS - 1) as c:
                    mlp_chunk(layer, c)
                if layer == 0:
                    pe.wait_ge(band_in_s, 16)
                mlp_chunk(layer, CHUNKS - 1, "last")
                if layer == 0:
                    def first_up_half(j):
                        up_group(mlp_bank(1, "first", j), w1_first[j], 0,
                                 [(w_lo, U_W1[1] + j + 1), (tr_lo, 2 * (TR_MLP1 + 3) + 2),
                                  (dn_used, DN_POOL + 2 * (NT - 3) + j + 1)], src=aT)

                    pe.wait_ge(w_lo, U_POOL + 2)
                    for t in range(NT):
                        pe.wait_ge(tr_lo, 2 * (TR_POOL + t) + 2)
                        for half in range(2):
                            g = DN_POOL + 2 * t + half
                            pe.wait_ge(dn_used, g - 1 if t == NT - 1 else g - 3)
                            for grp in (2 * half, 2 * half + 1):
                                c0 = (grp % 2) * 2 * P
                                pairs = [(parts(aT, 2 * grp + kt, t * P, P),
                                          tuple(a[:, grp * 2 * P:(grp + 1) * 2 * P] for a in (w_slot[kt].hi, w_slot[kt].lo))) for kt in range(2)]
                                mm = three_passes(pe, bank(pool_bank(t, half))[:, c0:c0 + 2 * P], pairs)
                            mm.then_inc(dn_full, 1)
                        if t == 0:
                            pe.wait_ge(xn_done, 3 * NT)
                            pool_tile(TR_POOL + 7, 7)
                        if t >= 2:
                            pe.wait_ge(xn_done, 3 * NT + t - 1)
                            transpose_tile(TR_MLP1 + t - 2, xn[t % 2])
                        if t == 6:
                            first_up_half(0)
                    pe.wait_ge(xn_done, 4 * NT - 1)
                    transpose_tile(TR_MLP1 + 6, xn[0])
                    first_up_half(1)
                    pe.wait_ge(xn_done, 4 * NT)
                    transpose_tile(TR_MLP1 + 7, xn[1])


_INS = ["x", "l0_norm_mix", "l0_fox_w_qkv", "l0_fox_w_f", "l0_fox_b_f", "l0_fox_w_o", "l0_norm_mlp", "l0_mlp_w1",
        "l0_mlp_w2", "l1_norm_mix", "l1_pool_w", "l1_pool_scale", "l1_norm_mlp", "l1_mlp_w1", "l1_mlp_w2", "final_norm"]


def kernel(**inputs):
    import concourse.bacc as _bacc
    from concourse.bass_utils import run_bass_kernel_spmd as _run

    nc = _bacc.Bacc("TRN2", target_bir_lowering=False, num_devices=1)
    arrays, args = {}, []
    values = {name: np.ascontiguousarray(inputs[name]) for name in _INS}
    values["const"], values["band"] = host_constants()
    for name, a in values.items():
        arrays[f"in_{name}"] = a
        args.append(nc.dram_tensor(f"in_{name}", a.shape, mybir.dt.from_np(a.dtype), kind="ExternalInput").ap())
    args.append(nc.dram_tensor("out", (1, T, D), F32, kind="ExternalOutput").ap())
    build(nc, *args)
    r = _run(nc, [arrays], core_ids=[0])
    return r.results[0]["out"]
```
